# Optimizing a Trainium2 kernel written in Bass

```python
import math
import jax, jax.numpy as jnp
from jax import lax
import numpy as np

D_MODEL = 1024
BATCH = 1
SEQ = 256
DEPTH = 2

MEM_LEN = 256
D_FF = 2816
LN_EPS = 1e-5
RMS_EPS = 1e-6
ROPE_THETA = 10000.0
DEEPNORM_ALPHA = (2 * DEPTH) ** 0.25
DEEPNORM_BETA = (8 * DEPTH) ** -0.25
Q_BLOCK = 128
NEG_INF = -1e30
N_BRANCHES = 4

GMLP_CHUNK = 128
GMLP_GROUPS = 4
GMLP_WIDTH = 512
GMLP_GROUP_DIM = GMLP_WIDTH // GMLP_GROUPS

CONV_WIDTH = 512
CONV_K = 3

MLA_HEADS = 8
MLA_Q_RANK = 256
MLA_KV_RANK = 128
MLA_NOPE = 64
MLA_ROPE = 32
MLA_V = 64

NSA_HEADS = 8
NSA_KV_GROUPS = 2
NSA_HPG = NSA_HEADS // NSA_KV_GROUPS
NSA_DIM = 64
NSA_KV_WIDTH = NSA_KV_GROUPS * NSA_DIM
CMP_BLOCK = 32
CMP_STRIDE = 16
SLC_BLOCK = 64
SLC_TOPK = 8
WINDOW = 512

XATTN_HEADS = 4
XATTN_DIM = 128

IN_SPLITS = (GMLP_WIDTH, GMLP_WIDTH,
             CONV_WIDTH, CONV_WIDTH, CONV_WIDTH,
             MLA_Q_RANK, MLA_KV_RANK, MLA_ROPE,
             NSA_HEADS * NSA_DIM) + (NSA_KV_WIDTH,) * 6 + (NSA_HEADS * 3,) + (D_MODEL,) * N_BRANCHES
IN_WIDTH = sum(IN_SPLITS)


def _layer_norm(x, g, b):
    xf = x.astype(jnp.float32)
    mu = jnp.mean(xf, -1, keepdims=True)
    var = jnp.mean(jnp.square(xf - mu), -1, keepdims=True)
    return ((xf - mu) * lax.rsqrt(var + LN_EPS) * g + b).astype(x.dtype)

def _rms_norm(x, g):
    xf = x.astype(jnp.float32)
    return (xf * lax.rsqrt(jnp.mean(xf * xf, -1, keepdims=True) + RMS_EPS) * g).astype(x.dtype)

def _rope_tables(pos, dim):
    inv = ROPE_THETA ** (-(jnp.arange(0, dim, 2, dtype=jnp.float32) / dim))
    ang = pos[:, None] * inv[None, :]
    return jnp.cos(ang), jnp.sin(ang)

def _apply_rope(x, cos, sin):
    x1, x2 = jnp.split(x.astype(jnp.float32), 2, axis=-1)
    return jnp.concatenate([x1 * cos - x2 * sin, x1 * sin + x2 * cos], -1).astype(x.dtype)

def _swiglu(x, w1, w3, w2):
    return (jax.nn.silu(x @ w1) * (x @ w3)) @ w2

def _blocked_causal_attention(q, k, v, scale):
    Bsz, S, H, dk = q.shape
    nq = S // Q_BLOCK
    qb = q.reshape(Bsz, nq, Q_BLOCK, H, dk).transpose(1, 0, 2, 3, 4)
    kpos = jnp.arange(S)

    def one(args):
        qi, blk = args
        qpos = blk * Q_BLOCK + jnp.arange(Q_BLOCK)
        s = jnp.einsum('bthd,bshd->bhts', qi, k).astype(jnp.float32) * scale
        s = jnp.where(kpos[None, :] <= qpos[:, None], s, NEG_INF)
        p = jax.nn.softmax(s, axis=-1).astype(v.dtype)
        return jnp.einsum('bhts,bshd->bthd', p, v)

    o = lax.map(one, (qb, jnp.arange(nq)))
    return o.transpose(1, 0, 2, 3, 4).reshape(Bsz, S, H, v.shape[-1])

def _gmlp_branch(u, v, ln_g, ln_b, w_s, b_s, w_out):
    Bsz, S, _ = u.shape
    n_chunk = S // GMLP_CHUNK
    v = _layer_norm(v, ln_g, ln_b).reshape(Bsz, n_chunk, GMLP_CHUNK, GMLP_GROUPS, GMLP_GROUP_DIM)
    causal = jnp.tril(jnp.ones((GMLP_CHUNK, GMLP_CHUNK), dtype=bool))
    w = jnp.where(causal, w_s, 0)
    s = jnp.einsum('gts,bcsgd->bctgd', w, v) + b_s.T[:, :, None]
    return (u * s.reshape(Bsz, S, GMLP_WIDTH)) @ w_out

def _short_conv_branch(b_gate, c_gate, h, conv_w, w_out):
    S = h.shape[1]
    zp = jnp.pad(c_gate * h, ((0, 0), (CONV_K - 1, 0), (0, 0)))
    y = zp[:, 0:S] * conv_w[0]
    for k in range(1, CONV_K):
        y = y + zp[:, k:k + S] * conv_w[k]
    return (b_gate * y) @ w_out

def _mla_branch(q_lat, kv_lat, k_rope, qn_g, kvn_g, w_uq, w_ukv, w_out, pos):
    Bsz, S, _ = q_lat.shape
    cos, sin = _rope_tables(pos, MLA_ROPE)
    q = (_rms_norm(q_lat, qn_g) @ w_uq).reshape(Bsz, S, MLA_HEADS, MLA_NOPE + MLA_ROPE)
    q = jnp.concatenate([q[..., :MLA_NOPE], _apply_rope(q[..., MLA_NOPE:], cos[:, None], sin[:, None])], -1)
    kv = (_rms_norm(kv_lat, kvn_g) @ w_ukv).reshape(Bsz, S, MLA_HEADS, MLA_NOPE + MLA_V)
    k_pe = _apply_rope(k_rope, cos, sin)[:, :, None, :]
    k = jnp.concatenate([kv[..., :MLA_NOPE], jnp.broadcast_to(k_pe, (Bsz, S, MLA_HEADS, MLA_ROPE))], -1)
    v = kv[..., MLA_NOPE:]
    o = _blocked_causal_attention(q, k, v, (MLA_NOPE + MLA_ROPE) ** -0.5)
    return o.reshape(Bsz, S, MLA_HEADS * MLA_V) @ w_out

def _nsa_branch(q, k_c, v_c, k_s, v_s, k_w, v_w, gate, pe_k, pe_v, wcmp_k, wcmp_v, w_out, pos):
    Bsz, S, _ = q.shape
    G, Hg, d = NSA_KV_GROUPS, NSA_HPG, NSA_DIM
    cos, sin = _rope_tables(pos, d)
    q = _apply_rope(q.reshape(Bsz, S, NSA_HEADS, d), cos[:, None], sin[:, None])
    k_c, v_c, k_s, v_s, k_w, v_w = [t.reshape(Bsz, S, G, d) for t in (k_c, v_c, k_s, v_s, k_w, v_w)]
    k_s = _apply_rope(k_s, cos[:, None], sin[:, None])
    k_w = _apply_rope(k_w, cos[:, None], sin[:, None])
    gate = jax.nn.sigmoid(gate).reshape(Bsz, S, NSA_HEADS, 3)

    n_cmp = (S - CMP_BLOCK) // CMP_STRIDE + 1
    cmp_start = jnp.arange(n_cmp) * CMP_STRIDE
    cmp_end = cmp_start + CMP_BLOCK - 1
    cmp_idx = cmp_start[:, None] + jnp.arange(CMP_BLOCK)[None, :]
    k_cmp = jnp.einsum('bnlgd,lde->bnge', k_c[:, cmp_idx] + pe_k[:, None, :], wcmp_k)
    v_cmp = jnp.einsum('bnlgd,lde->bnge', v_c[:, cmp_idx] + pe_v[:, None, :], wcmp_v)
    ccos, csin = _rope_tables(cmp_end.astype(jnp.float32), d)
    k_cmp = _apply_rope(k_cmp, ccos[:, None], csin[:, None])

    n_slc = S // SLC_BLOCK
    slc_start = jnp.arange(n_slc) * SLC_BLOCK
    ov = (jnp.minimum(cmp_start[:, None] + CMP_BLOCK, slc_start[None, :] + SLC_BLOCK)
          - jnp.maximum(cmp_start[:, None], slc_start[None, :]))
    overlap = jnp.clip(ov, 0).astype(jnp.float32) / CMP_BLOCK
    top_k = min(SLC_TOPK, n_slc)

    ks_blk = k_s.transpose(0, 2, 1, 3).reshape(Bsz, G, n_slc, SLC_BLOCK, d)
    vs_blk = v_s.transpose(0, 2, 1, 3).reshape(Bsz, G, n_slc, SLC_BLOCK, d)
    kw_pad = jnp.pad(k_w, ((0, 0), (WINDOW, 0), (0, 0), (0, 0)))
    vw_pad = jnp.pad(v_w, ((0, 0), (WINDOW, 0), (0, 0), (0, 0)))
    b_idx = jnp.arange(Bsz)[:, None, None, None]
    g_idx = jnp.arange(G)[None, :, None, None]
    scale = d ** -0.5
    jr = jnp.arange(n_slc)

    nq = S // Q_BLOCK
    qb = q.reshape(Bsz, nq, Q_BLOCK, G, Hg, d).transpose(1, 0, 2, 3, 4, 5)
    gb = gate.reshape(Bsz, nq, Q_BLOCK, G, Hg, 3).transpose(1, 0, 2, 3, 4, 5)

    def one(args):
        qi, g_blk, blk = args
        qpos = blk * Q_BLOCK + jnp.arange(Q_BLOCK)
        s = jnp.einsum('btghd,bngd->bghtn', qi, k_cmp).astype(jnp.float32) * scale
        valid = cmp_end[None, :] <= qpos[:, None]
        p_cmp = jnp.where(valid, jax.nn.softmax(jnp.where(valid, s, NEG_INF), axis=-1), 0.0)
        o_cmp = jnp.einsum('bghtn,bngd->btghd', p_cmp.astype(v_cmp.dtype), v_cmp)
        imp = jnp.einsum('bghtn,nj->bgtj', p_cmp, overlap)
        j_q = qpos // SLC_BLOCK
        forced = (jr[None, :] == 0) | (jr[None, :] == j_q[:, None]) | (jr[None, :] == j_q[:, None] - 1)
        imp = jnp.where(forced, 1e9, imp)
        imp = jnp.where(jr[None, :] <= j_q[:, None], imp, -1.0)
        top_s, top_i = lax.top_k(imp, top_k)
        k_sel = ks_blk[b_idx, g_idx, top_i].reshape(Bsz, G, Q_BLOCK, top_k * SLC_BLOCK, d)
        v_sel = vs_blk[b_idx, g_idx, top_i].reshape(Bsz, G, Q_BLOCK, top_k * SLC_BLOCK, d)
        tok = (top_i[..., None] * SLC_BLOCK + jnp.arange(SLC_BLOCK)).reshape(Bsz, G, Q_BLOCK, top_k * SLC_BLOCK)
        ok = (tok <= qpos[:, None]) & jnp.repeat(top_s >= 0, SLC_BLOCK, axis=-1)
        s = jnp.einsum('btghd,bgtnd->bghtn', qi, k_sel).astype(jnp.float32) * scale
        s = jnp.where(ok[:, :, None], s, NEG_INF)
        o_slc = jnp.einsum('bghtn,bgtnd->btghd', jax.nn.softmax(s, axis=-1).astype(v_sel.dtype), v_sel)
        k_win = lax.dynamic_slice_in_dim(kw_pad, blk * Q_BLOCK, WINDOW + Q_BLOCK, axis=1)
        v_win = lax.dynamic_slice_in_dim(vw_pad, blk * Q_BLOCK, WINDOW + Q_BLOCK, axis=1)
        kpos = blk * Q_BLOCK - WINDOW + jnp.arange(WINDOW + Q_BLOCK)
        dist = qpos[:, None] - kpos[None, :]
        okw = (dist >= 0) & (dist < WINDOW) & (kpos[None, :] >= 0)
        s = jnp.einsum('btghd,bsgd->bghts', qi, k_win).astype(jnp.float32) * scale
        s = jnp.where(okw, s, NEG_INF)
        o_win = jnp.einsum('bghts,bsgd->btghd', jax.nn.softmax(s, axis=-1).astype(v_win.dtype), v_win)
        return g_blk[..., 0:1] * o_cmp + g_blk[..., 1:2] * o_slc + g_blk[..., 2:3] * o_win

    o = lax.map(one, (qb, gb, jnp.arange(nq)))
    o = o.transpose(1, 0, 2, 3, 4, 5).reshape(Bsz, S, NSA_HEADS * d)
    return o @ w_out

def _token_mixing(h, w_in, b_in, gmlp_ln_g, gmlp_ln_b, gmlp_ws, gmlp_bs, gmlp_wout,
                  conv_w, conv_wout, mla_qnorm_g, mla_kvnorm_g, mla_wuq, mla_wukv, mla_wout,
                  nsa_pe_k, nsa_pe_v, nsa_wcmp_k, nsa_wcmp_v, nsa_wout, w_o):
    S = h.shape[1]
    z = h @ w_in + b_in
    offs = np.cumsum(IN_SPLITS)[:-1].tolist()
    (u, v, cb, cc, ch, q_lat, kv_lat, k_rope, nq, nkc, nvc, nks, nvs, nkw, nvw, ngate,
     ga, gb, gc, gd) = jnp.split(z, offs, axis=-1)
    pos = jnp.arange(S, dtype=jnp.float32)
    y_a = _gmlp_branch(u, v, gmlp_ln_g, gmlp_ln_b, gmlp_ws, gmlp_bs, gmlp_wout)
    y_b = _short_conv_branch(cb, cc, ch, conv_w, conv_wout)
    y_c = _mla_branch(q_lat, kv_lat, k_rope, mla_qnorm_g, mla_kvnorm_g, mla_wuq, mla_wukv, mla_wout, pos)
    y_d = _nsa_branch(nq, nkc, nvc, nks, nvs, nkw, nvw, ngate, nsa_pe_k, nsa_pe_v,
                      nsa_wcmp_k, nsa_wcmp_v, nsa_wout, pos)
    merged = (jax.nn.sigmoid(ga) * y_a + jax.nn.sigmoid(gb) * y_b
              + jax.nn.sigmoid(gc) * y_c + jax.nn.sigmoid(gd) * y_d)
    return merged @ w_o

def _cross_attention(x, mem, wq, wk, wv, wo):
    Bsz, S, _ = x.shape
    M = mem.shape[1]
    q = (x @ wq).reshape(Bsz, S, XATTN_HEADS, XATTN_DIM)
    k = (mem @ wk).reshape(Bsz, M, XATTN_HEADS, XATTN_DIM)
    v = (mem @ wv).reshape(Bsz, M, XATTN_HEADS, XATTN_DIM)
    s = jnp.einsum('bthd,bmhd->bhtm', q, k).astype(jnp.float32) * XATTN_DIM ** -0.5
    p = jax.nn.softmax(s, axis=-1).astype(v.dtype)
    o = jnp.einsum('bhtm,bmhd->bthd', p, v).reshape(Bsz, S, XATTN_HEADS * XATTN_DIM)
    return o @ wo

def first_inputs(seed: int = 0) -> dict:
    key = jax.random.key(seed)
    keys = iter(jax.random.split(key, 64))

    def dense(shape, fan_in, scale=1.0):
        return jax.random.normal(next(keys), (DEPTH,) + shape, jnp.float32) * (scale * fan_in ** -0.5)

    def gain(shape):
        return 1.0 + 0.02 * jax.random.normal(next(keys), (DEPTH,) + shape, jnp.float32)

    def small(shape, s=0.01):
        return s * jax.random.normal(next(keys), (DEPTH,) + shape, jnp.float32)

    D, F = D_MODEL, D_FF
    return {
        'x': jax.random.normal(next(keys), (BATCH, SEQ, D), jnp.float32),
        'mem': jax.random.normal(next(keys), (BATCH, MEM_LEN, D), jnp.float32),
        'ffn1_w1': dense((D, F), D),
        'ffn1_w3': dense((D, F), D),
        'ffn1_w2': dense((F, D), F, DEEPNORM_BETA),
        'ln1_g': gain((D,)),
        'ln1_b': small((D,)),
        'w_in': dense((D, IN_WIDTH), D),
        'b_in': small((IN_WIDTH,)),
        'gmlp_ln_g': gain((GMLP_WIDTH,)),
        'gmlp_ln_b': small((GMLP_WIDTH,)),
        'gmlp_ws': dense((GMLP_GROUPS, GMLP_CHUNK, GMLP_CHUNK), GMLP_CHUNK),
        'gmlp_bs': gain((GMLP_GROUPS, GMLP_CHUNK)),
        'gmlp_wout': dense((GMLP_WIDTH, D), GMLP_WIDTH),
        'conv_w': dense((CONV_K, CONV_WIDTH), CONV_K),
        'conv_wout': dense((CONV_WIDTH, D), CONV_WIDTH),
        'mla_qnorm_g': gain((MLA_Q_RANK,)),
        'mla_kvnorm_g': gain((MLA_KV_RANK,)),
        'mla_wuq': dense((MLA_Q_RANK, MLA_HEADS * (MLA_NOPE + MLA_ROPE)), MLA_Q_RANK),
        'mla_wukv': dense((MLA_KV_RANK, MLA_HEADS * (MLA_NOPE + MLA_V)), MLA_KV_RANK),
        'mla_wout': dense((MLA_HEADS * MLA_V, D), MLA_HEADS * MLA_V),
        'nsa_pe_k': small((CMP_BLOCK, NSA_DIM), 0.02),
        'nsa_pe_v': small((CMP_BLOCK, NSA_DIM), 0.02),
        'nsa_wcmp_k': dense((CMP_BLOCK, NSA_DIM, NSA_DIM), CMP_BLOCK * NSA_DIM),
        'nsa_wcmp_v': dense((CMP_BLOCK, NSA_DIM, NSA_DIM), CMP_BLOCK * NSA_DIM),
        'nsa_wout': dense((NSA_HEADS * NSA_DIM, D), NSA_HEADS * NSA_DIM),
        'w_o': dense((D, D), D, DEEPNORM_BETA),
        'ln2_g': gain((D,)),
        'ln2_b': small((D,)),
        'xattn_wq': dense((D, XATTN_HEADS * XATTN_DIM), D),
        'xattn_wk': dense((D, XATTN_HEADS * XATTN_DIM), D),
        'xattn_wv': dense((D, XATTN_HEADS * XATTN_DIM), D),
        'xattn_wo': dense((XATTN_HEADS * XATTN_DIM, D), XATTN_HEADS * XATTN_DIM, DEEPNORM_BETA),
        'ln3_g': gain((D,)),
        'ln3_b': small((D,)),
        'ffn2_w1': dense((D, F), D),
        'ffn2_w3': dense((D, F), D),
        'ffn2_w2': dense((F, D), F, DEEPNORM_BETA),
        'ln4_g': gain((D,)),
        'ln4_b': small((D,)),
    }

def first_block(x, mem, ffn1_w1, ffn1_w3, ffn1_w2, ln1_g, ln1_b, w_in, b_in,
              gmlp_ln_g, gmlp_ln_b, gmlp_ws, gmlp_bs, gmlp_wout, conv_w, conv_wout,
              mla_qnorm_g, mla_kvnorm_g, mla_wuq, mla_wukv, mla_wout,
              nsa_pe_k, nsa_pe_v, nsa_wcmp_k, nsa_wcmp_v, nsa_wout,
              w_o, ln2_g, ln2_b, xattn_wq, xattn_wk, xattn_wv, xattn_wo, ln3_g, ln3_b,
              ffn2_w1, ffn2_w3, ffn2_w2, ln4_g, ln4_b):
    a = DEEPNORM_ALPHA
    for l in range(DEPTH):
        x = _layer_norm(a * x + 0.5 * _swiglu(x, ffn1_w1[l], ffn1_w3[l], ffn1_w2[l]), ln1_g[l], ln1_b[l])
        mix = _token_mixing(x, w_in[l], b_in[l], gmlp_ln_g[l], gmlp_ln_b[l], gmlp_ws[l], gmlp_bs[l],
                            gmlp_wout[l], conv_w[l], conv_wout[l], mla_qnorm_g[l], mla_kvnorm_g[l],
                            mla_wuq[l], mla_wukv[l], mla_wout[l], nsa_pe_k[l], nsa_pe_v[l],
                            nsa_wcmp_k[l], nsa_wcmp_v[l], nsa_wout[l], w_o[l])
        x = _layer_norm(a * x + mix, ln2_g[l], ln2_b[l])
        x = _layer_norm(a * x + _cross_attention(x, mem, xattn_wq[l], xattn_wk[l], xattn_wv[l], xattn_wo[l]),
                        ln3_g[l], ln3_b[l])
        x = _layer_norm(a * x + 0.5 * _swiglu(x, ffn2_w1[l], ffn2_w3[l], ffn2_w2[l]), ln4_g[l], ln4_b[l])
    return x


CHUNK = 64
EPS = 1e-6
PLE_DIM = 256
FFN_RES = 0.5
N_EVEN = (DEPTH + 1) // 2
N_ODD = DEPTH // 2

GLA_HEADS = 4
GLA_V = D_MODEL // 2
GLA_DV = GLA_V // GLA_HEADS
GLA_QK = GLA_V // 2
GLA_DK = GLA_QK // GLA_HEADS
GLA_RANK = 16
GLA_GATE_TEMP = 16.0

LRU_WIDTH = D_MODEL // 2
LRU_BLOCKS = 8
LRU_BW = LRU_WIDTH // LRU_BLOCKS
CONV_W = 4
LRU_C = 8.0

MIX0_SPLITS = [int(c) for c in np.cumsum([GLA_QK, GLA_QK, GLA_V, GLA_V, GLA_RANK, LRU_WIDTH])]
MIX0_COLS = 2 * GLA_QK + 2 * GLA_V + GLA_RANK + 2 * LRU_WIDTH
MIX0_OUT = GLA_V + LRU_WIDTH

HG_DK = 128
HG_HEADS = D_MODEL // HG_DK
HG_DV = 128
HG_K = HG_HEADS * HG_DK
HG_V = HG_HEADS * HG_DV
MIX1_SPLITS = [HG_K, 2 * HG_K, 2 * HG_K + HG_V]
MIX1_COLS = 2 * HG_K + 2 * HG_V


def rmsnorm(x, g):
    xf = x.astype(jnp.float32)
    y = xf * lax.rsqrt(jnp.mean(xf * xf, axis=-1, keepdims=True) + EPS)
    return (y * g.astype(jnp.float32)).astype(x.dtype)

def swiglu(h, w1, w3, w2):
    return (jax.nn.silu(h @ w1) * (h @ w3)) @ w2

def chunk_end_gated_linear_attention(q, k, v, log_f):
    b, s, h, dk = q.shape
    dv = v.shape[-1]
    n = s // CHUNK

    def chunks(t):
        return jnp.moveaxis(t.astype(jnp.float32).reshape(b, n, CHUNK, h, t.shape[-1]), 1, 0)

    qc, kc, vc, lf = chunks(q), chunks(k), chunks(v), chunks(log_f)
    cum = jnp.cumsum(lf, axis=2)
    total = cum[:, :, -1]
    k_dec = kc * jnp.exp(total[:, :, None] - cum)
    g_chunk = jnp.exp(total)

    def step(state, xs):
        q_c, k_c, v_c, g_c = xs
        state = g_c[..., None] * state + jnp.einsum('bchk,bchv->bhkv', k_c, v_c)
        return state, jnp.einsum('bchk,bhkv->bchv', q_c, state)

    s0 = jnp.zeros((b, h, dk, dv), jnp.float32)
    _, o = lax.scan(step, s0, (qc, k_dec, vc, g_chunk))
    return jnp.moveaxis(o, 0, 1).reshape(b, s, h, dv).astype(v.dtype)

def causal_depthwise_conv(x, w, bias):
    s = x.shape[1]
    xp = jnp.pad(x, ((0, 0), (CONV_W - 1, 0), (0, 0)))
    out = xp[:, 0:s] * w[0]
    for j in range(1, CONV_W):
        out = out + xp[:, j:j + s] * w[j]
    return out + bias

def block_diag(x, w, bias):
    b, s, wd = x.shape
    xb = x.reshape(b, s, LRU_BLOCKS, LRU_BW)
    return jnp.einsum('bsgi,gij->bsgj', xb, w).reshape(b, s, wd) + bias

def rg_lru(x, w_a, b_a, w_x, b_x, lam):
    r = jax.nn.sigmoid(block_diag(x, w_a, b_a)).astype(jnp.float32)
    i = jax.nn.sigmoid(block_diag(x, w_x, b_x))
    log_a = LRU_C * r * jax.nn.log_sigmoid(lam.astype(jnp.float32))
    a = jnp.exp(log_a)
    u = jnp.sqrt(-jnp.expm1(2.0 * log_a)) * (i * x).astype(jnp.float32)

    def combine(left, right):
        a1, b1 = left
        a2, b2 = right
        return a1 * a2, a2 * b1 + b2

    _, hs = lax.associative_scan(combine, (a, u), axis=1)
    return hs.astype(x.dtype)

def mixer_gla_rglru(h, w_in, gla_gate_up, gla_gate_bias, gla_head_norm, conv_w, conv_b,
                    lru_wa, lru_ba, lru_wx, lru_bx, lru_lambda, w_out):
    b, s, _ = h.shape
    z = h @ w_in
    q, k, v, g, lr, xr, xg = jnp.split(z, MIX0_SPLITS, axis=-1)
    log_f = jax.nn.log_sigmoid((lr @ gla_gate_up + gla_gate_bias).astype(jnp.float32)) / GLA_GATE_TEMP
    o = chunk_end_gated_linear_attention(
        q.reshape(b, s, GLA_HEADS, GLA_DK) * (GLA_DK ** -0.5),
        k.reshape(b, s, GLA_HEADS, GLA_DK),
        v.reshape(b, s, GLA_HEADS, GLA_DV),
        log_f.reshape(b, s, GLA_HEADS, GLA_DK))
    o = rmsnorm(o, gla_head_norm).reshape(b, s, GLA_V) * jax.nn.silu(g)
    y = rg_lru(causal_depthwise_conv(xr, conv_w, conv_b), lru_wa, lru_ba, lru_wx, lru_bx, lru_lambda)
    y = y * jax.nn.gelu(xg)
    return jnp.concatenate([o, y], axis=-1) @ w_out

def mixer_hgrn2(h, w_in, lb, hg_head_norm, w_out):
    b, s, _ = h.shape
    z = h @ w_in
    q, fz, i, g = jnp.split(z, MIX1_SPLITS, axis=-1)
    lbf = lb.astype(jnp.float32)
    zf = fz.astype(jnp.float32)
    log_f = jnp.logaddexp(jnp.log(lbf), jnp.log1p(-lbf) + jax.nn.log_sigmoid(zf))
    k = (1.0 - lbf) * jax.nn.sigmoid(-zf)
    o = chunk_end_gated_linear_attention(
        jax.nn.silu(q).reshape(b, s, HG_HEADS, HG_DK),
        k.astype(h.dtype).reshape(b, s, HG_HEADS, HG_DK),
        i.reshape(b, s, HG_HEADS, HG_DV),
        log_f.reshape(b, s, HG_HEADS, HG_DK))
    o = rmsnorm(o, hg_head_norm).reshape(b, s, HG_V) * jax.nn.silu(g)
    return o @ w_out

def lower_bounds(lb_logits):
    sm = jax.nn.softmax(lb_logits.astype(jnp.float32), axis=0)
    return jnp.cumsum(sm, axis=0) - sm[0]

def half_ffn(x, g, w1, w3, w2):
    return x + FFN_RES * swiglu(rmsnorm(x, g), w1, w3, w2)

def second_inputs(seed: int = 0) -> dict:
    key = jax.random.key(seed)
    ks = iter(list(jax.random.split(key, 40)))

    def nrm(shape, scale):
        return jax.random.normal(next(ks), shape, jnp.float32) * scale

    def gain(shape):
        return 1.0 + nrm(shape, 0.05)

    a0 = jax.random.uniform(next(ks), (N_EVEN, LRU_WIDTH), jnp.float32, 0.9, 0.999)
    return {
        'x': nrm((BATCH, SEQ, D_MODEL), 1.0),
        'p': nrm((DEPTH, BATCH, SEQ, PLE_DIM), 1.0),
        'ffn_norm': gain((DEPTH, 2, D_MODEL)),
        'ffn_w1': nrm((DEPTH, 2, D_MODEL, D_FF), D_MODEL ** -0.5),
        'ffn_w3': nrm((DEPTH, 2, D_MODEL, D_FF), D_MODEL ** -0.5),
        'ffn_w2': nrm((DEPTH, 2, D_FF, D_MODEL), D_FF ** -0.5),
        'mix_norm': gain((DEPTH, D_MODEL)),
        'ple_norm': gain((DEPTH, D_MODEL)),
        'ple_proj': nrm((DEPTH, PLE_DIM, D_MODEL), PLE_DIM ** -0.5),
        'ple_gate': nrm((DEPTH, D_MODEL, D_MODEL), D_MODEL ** -0.5),
        'final_norm': gain((D_MODEL,)),
        'm0_w_in': nrm((N_EVEN, D_MODEL, MIX0_COLS), D_MODEL ** -0.5),
        'gla_gate_up': nrm((N_EVEN, GLA_RANK, GLA_QK), GLA_RANK ** -0.5),
        'gla_gate_bias': nrm((N_EVEN, GLA_QK), 0.1),
        'gla_head_norm': gain((N_EVEN, GLA_DV)),
        'lru_conv_w': nrm((N_EVEN, CONV_W, LRU_WIDTH), CONV_W ** -0.5),
        'lru_conv_b': nrm((N_EVEN, LRU_WIDTH), 0.02),
        'lru_wa': nrm((N_EVEN, LRU_BLOCKS, LRU_BW, LRU_BW), LRU_BW ** -0.5),
        'lru_ba': nrm((N_EVEN, LRU_WIDTH), 0.02),
        'lru_wx': nrm((N_EVEN, LRU_BLOCKS, LRU_BW, LRU_BW), LRU_BW ** -0.5),
        'lru_bx': nrm((N_EVEN, LRU_WIDTH), 0.02),
        'lru_lambda': jnp.log(a0) - jnp.log1p(-a0),
        'm0_w_out': nrm((N_EVEN, MIX0_OUT, D_MODEL), MIX0_OUT ** -0.5),
        'm1_w_in': nrm((N_ODD, D_MODEL, MIX1_COLS), D_MODEL ** -0.5),
        'hgrn_lb_logits': nrm((DEPTH, HG_K), 0.1),
        'hgrn_head_norm': gain((N_ODD, HG_DV)),
        'm1_w_out': nrm((N_ODD, HG_V, D_MODEL), HG_V ** -0.5),
    }

def second_block(x, p, ffn_norm, ffn_w1, ffn_w3, ffn_w2, mix_norm, ple_norm, ple_proj, ple_gate,
              final_norm, m0_w_in, gla_gate_up, gla_gate_bias, gla_head_norm, lru_conv_w,
              lru_conv_b, lru_wa, lru_ba, lru_wx, lru_bx, lru_lambda, m0_w_out, m1_w_in,
              hgrn_lb_logits, hgrn_head_norm, m1_w_out):
    lbs = lower_bounds(hgrn_lb_logits)
    for layer in range(DEPTH):
        x = half_ffn(x, ffn_norm[layer, 0], ffn_w1[layer, 0], ffn_w3[layer, 0], ffn_w2[layer, 0])
        h = rmsnorm(x, mix_norm[layer])
        if layer % 2 == 0:
            e = layer // 2
            x = x + mixer_gla_rglru(h, m0_w_in[e], gla_gate_up[e], gla_gate_bias[e], gla_head_norm[e],
                                    lru_conv_w[e], lru_conv_b[e], lru_wa[e], lru_ba[e], lru_wx[e],
                                    lru_bx[e], lru_lambda[e], m0_w_out[e])
        else:
            o = layer // 2
            x = x + mixer_hgrn2(h, m1_w_in[o], lbs[layer], hgrn_head_norm[o], m1_w_out[o])
        x = half_ffn(x, ffn_norm[layer, 1], ffn_w1[layer, 1], ffn_w3[layer, 1], ffn_w2[layer, 1])
        gate = jax.nn.sigmoid(rmsnorm(x, ple_norm[layer]) @ ple_gate[layer])
        x = x + gate * (p[layer] @ ple_proj[layer])
    return rmsnorm(x, final_norm)


def setup_inputs(seed=0):
    out = dict(first_inputs(seed))
    for name, value in second_inputs(seed + 1).items():
        if name != "x":
            out[name + "_2"] = value
    return out


def reference(
    x, mem, ffn1_w1, ffn1_w3, ffn1_w2, ln1_g, ln1_b, w_in, b_in, gmlp_ln_g, gmlp_ln_b, gmlp_ws,
    gmlp_bs, gmlp_wout, conv_w, conv_wout, mla_qnorm_g, mla_kvnorm_g, mla_wuq, mla_wukv,
    mla_wout, nsa_pe_k, nsa_pe_v, nsa_wcmp_k, nsa_wcmp_v, nsa_wout, w_o, ln2_g, ln2_b, xattn_wq,
    xattn_wk, xattn_wv, xattn_wo, ln3_g, ln3_b, ffn2_w1, ffn2_w3, ffn2_w2, ln4_g, ln4_b, p_2,
    ffn_norm_2, ffn_w1_2, ffn_w3_2, ffn_w2_2, mix_norm_2, ple_norm_2, ple_proj_2, ple_gate_2,
    final_norm_2, m0_w_in_2, gla_gate_up_2, gla_gate_bias_2, gla_head_norm_2, lru_conv_w_2,
    lru_conv_b_2, lru_wa_2, lru_ba_2, lru_wx_2, lru_bx_2, lru_lambda_2, m0_w_out_2, m1_w_in_2,
    hgrn_lb_logits_2, hgrn_head_norm_2, m1_w_out_2,
):
    x = first_block(
        x, mem, ffn1_w1, ffn1_w3, ffn1_w2, ln1_g, ln1_b, w_in, b_in, gmlp_ln_g, gmlp_ln_b,
        gmlp_ws, gmlp_bs, gmlp_wout, conv_w, conv_wout, mla_qnorm_g, mla_kvnorm_g, mla_wuq,
        mla_wukv, mla_wout, nsa_pe_k, nsa_pe_v, nsa_wcmp_k, nsa_wcmp_v, nsa_wout, w_o, ln2_g,
        ln2_b, xattn_wq, xattn_wk, xattn_wv, xattn_wo, ln3_g, ln3_b, ffn2_w1, ffn2_w3, ffn2_w2,
        ln4_g, ln4_b,
    )
    return second_block(
        x, p_2, ffn_norm_2, ffn_w1_2, ffn_w3_2, ffn_w2_2, mix_norm_2, ple_norm_2, ple_proj_2,
        ple_gate_2, final_norm_2, m0_w_in_2, gla_gate_up_2, gla_gate_bias_2, gla_head_norm_2,
        lru_conv_w_2, lru_conv_b_2, lru_wa_2, lru_ba_2, lru_wx_2, lru_bx_2, lru_lambda_2,
        m0_w_out_2, m1_w_in_2, hgrn_lb_logits_2, hgrn_head_norm_2, m1_w_out_2,
    )


_drawn_inputs = setup_inputs


def setup_inputs(seed=0):
    import zlib

    import numpy as np

    out = dict(_drawn_inputs(seed))
    spreads = {}
    factors = {'b_in': 5.232,
     'gmlp_ln_g': 8.0,
     'gmlp_ln_b': 8.0,
     'gmlp_bs': 8.0,
     'mla_qnorm_g': 8.0,
     'mla_kvnorm_g': 8.0,
     'nsa_pe_k': 25.384,
     'nsa_pe_v': 8.0,
     'ple_norm_2': 14.339,
     'gla_gate_bias_2': 3.507,
     'gla_head_norm_2': 3.908,
     'lru_conv_b_2': 3.083,
     'lru_ba_2': 64.0,
     'lru_bx_2': 42.167,
     'hgrn_lb_logits_2': 8.0,
     'hgrn_head_norm_2': 2.842}
    for name, (base, spread) in spreads.items():
        noise = np.random.default_rng([zlib.crc32(name.encode()), seed]).standard_normal(out[name].shape)
        drawn = base * np.exp(spread * noise) if base else spread * noise
        out[name] = __import__('jax').numpy.asarray(drawn.astype(out[name].dtype))
    for name, factor in factors.items():
        out[name] = (out[name] * factor).astype(out[name].dtype)
    return out
```

```python
from contextlib import ExitStack

import numpy as np

import concourse.bass as bass
from concourse import mybir

P = 128
F32 = mybir.dt.float32
F32R = mybir.dt.float32r
BF16 = mybir.dt.bfloat16
ACT = mybir.ActivationFunctionType
ALU = mybir.AluOpType
AX = mybir.AxisListType

D = 1024
T = 256
DC = D // P
TT = T // P
FF = 2816
FC = FF // P
DEPTH = 2
ALPHA = float((2 * DEPTH) ** 0.25)
LN_EPS, RMS_EPS = 1e-5, 1e-6
N_CMP, CMP = 15, 16
NEG = -1e30

Z_KC, Z_VC, Z_KS, Z_VS, Z_KW, Z_VW, Z_Q, Z_MISC, Z_QL, Z_KVL = 0, 1, 2, 3, 4, 5, 6, 10, 11, 13
Z_U, Z_V, Z_CB, Z_CC, Z_CH, Z_N = 14, 18, 22, 26, 30, 34
Z_GATES = 4 * DC

RAW = 6
SPLIT = 4
BODY = 12
RING = 4


def mixer0_chunks():
    return dict(xr=0, xg=4, q=8, k=10, g=12, lr=16, n=17)


def count_blocks():
    ffn = 3 * FC
    first = (2 * ffn + Z_N + 3 + Z_GATES + 4 * 4 + DC
             + 4 + 4 + 4 + 4)
    second = 2 * ffn + DC + 2
    mix0 = 17 + 4 + 1 + DC
    mix1 = 8 + 8 + 8 + 8 + DC
    return DEPTH * first + DEPTH * second + mix0 + mix1


def column_plan():
    plan, at = {}, 0
    sizes = []
    for l in range(DEPTH):
        sizes += [(f"ln{i}_{k}{l}", DC) for i in range(1, 5) for k in "gb"]
        sizes += [(f"b_in{l}", Z_N + Z_GATES), (f"gln_g{l}", 4), (f"gln_b{l}", 4), (f"conv{l}", 12),
                  (f"qn{l}", 2), (f"kvn{l}", 1), (f"pe_k{l}", 32), (f"pe_v{l}", 32)]
        sizes += [(f"ffn_g{l}_{i}", DC) for i in range(2)] + [(f"mix_g{l}", DC), (f"ple_g{l}", DC),
                                                              (f"lb{l}", DC)]
    sizes += [("final_g", DC), ("gate_up", 256), ("gate_b", 2), ("gla_hn", 1), ("lconv", 16), ("lconv_b", 4),
              ("lru_ba", 4), ("lru_bx", 4), ("lam", 4), ("hg_hn", 1)]
    for name, n in sizes:
        plan[name] = (at, n)
        at += n
    return plan, at


def table_plan():
    plan, at = {}, 0
    for name, n in [("ones", P), ("ident", P), ("perm64", P), ("place", P), ("tri", P), ("sel16", P),
                    ("vmask", 4 * P), ("cos64", T), ("sin64", T), ("tqe", T), ("tqo", T), ("reset", T),
                    ("ccos", CMP), ("csin", CMP), ("valid", 2 * CMP)]:
        plan[name] = (at, n)
        at += n
    return plan, at


def tables():
    plan, n = table_plan()
    out = np.zeros((P, n), np.float32)

    def put(name, a):
        a = np.asarray(a, np.float32).reshape(a.shape[0], -1)
        out[:a.shape[0], plan[name][0]:plan[name][0] + plan[name][1]] = a

    p = np.arange(P)

    def angles(pos, dim):
        inv = (np.float32(10000.0) ** (-(np.arange(0, dim, 2, dtype=np.float32) / dim))).astype(np.float32)
        a = (pos.astype(np.float32)[:, None] * inv[None, :]).astype(np.float32)
        c, s = np.cos(a).T, np.sin(a).T
        return np.concatenate([c, c]), np.concatenate([-s, s])

    put("ones", np.ones((P, P)))
    put("ident", np.eye(P))
    put("perm64", (p[:, None] // 64 == p[None] // 64) & ((p[:, None] + 32) % 64 == p[None] % 64))
    put("place", p[:64, None] % 32 == p[None] % 32)
    put("tri", p[:, None] <= p[None])
    put("sel16", p[:CMP, None] == p[None] % CMP)
    vm = np.zeros((P, 4, 2, 64))
    for h in range(8):
        vm[h * CMP:h * CMP + N_CMP, h % 4, h // 4] = 1
    put("vmask", vm)
    c, s = angles(np.arange(T), 64)
    put("cos64", np.concatenate([c, c]))
    put("sin64", np.concatenate([s, s]))
    c, s = angles(np.arange(T), 32)
    one = np.ones((64, T))
    put("tqe", np.concatenate([one, c, s]))
    put("tqo", np.concatenate([c, s, one]))
    put("reset", np.broadcast_to(np.arange(T) % 64 != 0, (P, T)))
    ends = np.arange(N_CMP) * 16 + 31
    c, s = angles(ends, 64)
    pad = np.zeros((64, 1))
    c, s = np.concatenate([c, pad], 1), np.concatenate([s, pad], 1)
    put("ccos", np.concatenate([c, c]))
    put("csin", np.concatenate([s, s]))
    q = p[:, None] + P * np.arange(TT)[None]
    valid = np.zeros((P, TT, CMP))
    valid[:, :, :N_CMP] = ends[None, None] <= q[:, :, None]
    put("valid", valid)
    after = (p[None] > p[:, None]) * NEG
    masks = np.zeros((P, 2 * T), np.float32)
    masks[:, 0:3 * P] = np.concatenate([after, 0 * after, after], 1)
    masks[:, 3 * P:] = np.repeat(((1 - valid) * NEG)[:, :, None], 4, 2).reshape(P, -1)
    return out, masks


class Tally:

    def __init__(self):
        self.n, self.it, self.per = {}, None, {}

    def value(self, key):
        v = self.n.get(key, 0)
        return v if self.it is None else self.it * self.per[key] + v

    def up(self, key, k=1):
        self.n[key] = self.n.get(key, 0) + k
        return self.value(key)

    def enter(self, it, per):
        self.it, self.per, self.start = it, per, dict(self.n)

    def leave(self, trips):
        for key, k in self.per.items():
            grown = self.n.get(key, 0) - self.start.get(key, 0)
            assert grown == k, (key, grown, k)
            self.n[key] = self.start.get(key, 0) + k * trips
        grown = {k for k in self.n if self.n[k] != self.start.get(k, 0)}
        assert grown <= set(self.per), grown - set(self.per)
        self.it, self.per = None, {}


def build_program(nc, stream, small, table, masks, mix_w, mix_b, wcmp, x_in, mem_in, p_in, out):
    NB = count_blocks()
    cols, n_cols = column_plan()
    tabs, n_tabs = table_plan()
    ctx = ExitStack()
    with ctx:
        def sb(name, shape, dt=F32):
            return ctx.enter_context(nc.sbuf_tensor(name, shape, dt))

        def sem(name):
            return ctx.enter_context(nc.semaphore(name))

        raw = sb("raw", [P, RAW, 1024])
        wh = sb("wh", [P, SPLIT, 1024], F32R)
        wl = sb("wl", [P, SPLIT, 1024], F32R)
        X = sb("X", [P, DC, T])
        XH = sb("XH", [P, DC, T], F32R)
        XL = sb("XL", [P, DC, T], F32R)
        W8 = sb("W8", [P, DC, T])
        M = sb("M", [P, DC, T])
        Z = sb("Z", [P, Z_N, T])
        G = sb("G", [P, 2, DC, T])
        BH = sb("BH", [P, DC, T], F32R)
        BL = sb("BL", [P, DC, T], F32R)
        O = sb("O", [P, 4, T])
        PR = sb("PR", [P, 2, 512])
        PTS = sb("PTS", [P, 2, 512])
        VSW = sb("VSW", [P, 4, P])
        SM = sb("SM", [P, n_cols])
        TB = sb("TB", [P, n_tabs])
        CAUS = sb("CAUS", [P, 3 * P], BF16)
        CMSK = sb("CMSK", [P, 2, 4 * CMP], BF16)
        IDB = sb("IDB", [P, P], BF16)
        ZB = sb("ZB", [P, 512], BF16)
        WS = sb("WS", [P, 4, P])
        S1 = sb("S1", [P, T])
        S2 = sb("S2", [P, 512])
        S3 = sb("S3", [P, 512])
        S4 = sb("S4", [P, 512])
        EPS = sb("EPS", [P, 3])
        NB_IN = sb("NB_IN", [P, Z_GATES])
        GT = sb("GT", [P, 2, 24])
        mx = sb("mx", [P, 2, 2])
        nm = sb("nm", [P, 2, 2])
        ls = sb("ls", [P, 2, 2])
        rl = sb("rl", [P, 2, 2])
        KC = sb("KC", [P, 2, CMP])
        VCs = sb("VCs", [CMP, P])
        VCB = sb("VCB", [P, 4, P])
        c8 = sb("c8", [P, 6, 8])
        LB = sb("LB", [P, 3, DC])

        Y = ctx.enter_context(nc.psum_tensor("Y", [P, 4, 512], F32))
        R = ctx.enter_context(nc.psum_tensor("R", [P, RING, 512], F32))

        raw_landed = [sem(f"raw_landed{i}") for i in range(RAW)]
        hi_done, lo_done, block_begun = sem("hi_done"), sem("lo_done"), sem("block_begun")
        chunk_ready = sem("chunk_ready")
        bank_taken = [sem(f"bank_taken{i}") for i in range(RING)]
        small_landed, x_landed, wcmp_landed = sem("small_landed"), sem("x_landed"), sem("wcmp_landed")
        mix_landed, in_landed = sem("mix_landed"), sem("in_landed")
        act_step, dve_step = sem("act_step"), sem("dve_step")
        dve_act, dve_pe, act_dve, act_pe = sem("dve_act"), sem("dve_pe"), sem("act_dve"), sem("act_pe")
        scores_ready, pt_ready, o_ready, o_taken, y_ready = (sem("scores_ready"), sem("pt_ready"), sem("o_ready"),
                                                             sem("o_taken"), sem("y_ready"))
        out_stored, pool_const = sem("out_stored"), sem("pool_const")

        def col(name, i=0, k=1):
            a = cols[name][0]
            return SM[:, a + i:a + i + k]

        def tab(name, rows=P):
            a, n = tabs[name]
            return TB[0:rows, a:a + n]

        ONES, IDF = tab("ones"), tab("ident")
        QM = Z[:, Z_CB:Z_CB + 8, :]
        VM = Z[:, Z_CH:Z_CH + 4, :].rearrange("p (a b) t -> p a (b t)", a=2)
        KM = M
        BSR = PTS[0:1, 1, :]
        WC = G[:, :, :, :].rearrange("p a c t -> p a (c t)")
        HH, HL = BH, BL
        EB = M
        HID = W8

        def mla_unit(h):
            return dict(q=QM[:, h, :], k=KM[:, h, :], v=lambda kt: VM[:, kt, h * 64:h * 64 + 64], row=64 * (h % 2), width=64,
                        c=h // 2, first=True, last=h % 2 == 1, opens=h % 2 == 0, gate=None, scale=96 ** -0.5, full=False)

        def nsa_unit(u):
            c, br, g = u // 4, u // 2 % 2, u % 2
            k = Z_KS if br == 0 else Z_KW
            s = slice(64 * g, 64 * g + 64)
            return dict(q=Z[s, Z_Q + c, :], k=Z[s, k, :], v=lambda kt: VSW[:, 2 * br + kt, s], row=64 * g, width=64, c=c,
                        first=False, last=u % 4 == 3, opens=u % 4 == 0, gate=3 * (4 * g + c) + 1 + br, scale=0.125, full=False)

        def cross_unit(h):
            return dict(q=Z[:, 4 + h, :], k=Z[:, h, :], v=lambda kt: Z[:, 8 + 2 * kt:10 + 2 * kt, :].rearrange(
                "p a t -> p (a t)")[:, h * P:h * P + P], row=0, width=P, c=h, first=True, last=True, opens=True, gate=None,
                scale=P ** -0.5, full=True)

        block = ctx.enter_context(nc.Block())

        @block.sync
        def _(sp):
            sp.dma_start(SM[:, :], small).then_inc(small_landed, 16)
            sp.dma_start(TB[:, :], table).then_inc(small_landed, 16)
            sp.dma_start(Z[:, 0:2, :], masks).then_inc(small_landed, 16)
            sp.dma_start(X[:, :, :], x_in).then_inc(x_landed, 16)
            for n in range(RAW):
                sp.dma_start(raw[:, n, :], stream[n]).then_inc(raw_landed[n], 16)
            trips = (NB - RAW) // RAW
            with sp.Fori(0, trips) as it:
                for j in range(RAW):
                    sp.wait_ge(lo_done, it * RAW + (j + 1))
                    sp.dma_start(raw[:, j, :], stream[it * RAW + (RAW + j)]).then_inc(raw_landed[j], 16)
            for n in range(RAW + trips * RAW, NB):
                sp.wait_ge(lo_done, n - RAW + 1)
                sp.dma_start(raw[:, n % RAW, :], stream[n]).then_inc(raw_landed[n % RAW], 16)

        @block.gpsimd
        def _(pool):
            pool.memset(ZB[:, :], 0.0).then_inc(pool_const, 1)
            pool.memset(EPS[:, 0:1], LN_EPS).then_inc(pool_const, 1)
            pool.memset(EPS[:, 1:2], RMS_EPS).then_inc(pool_const, 1)
            pool.memset(EPS[:, 2:3], 1.0).then_inc(pool_const, 1)

            def low(j):
                r, s = j % RAW, j % SPLIT
                pool.tensor_tensor(wl[:, s, :], raw[:, r, :], wh[:, s, :].bitcast(F32), ALU.subtract).then_inc(lo_done, 1)

            trips = NB // BODY
            with pool.Fori(0, trips) as it:
                for j in range(BODY):
                    pool.wait_ge(hi_done, it * BODY + (j + 1))
                    low(j)
            for n in range(trips * BODY, NB):
                pool.wait_ge(hi_done, n + 1)
                low(n)

        @block.tensor
        def _(pe):
            t = Tally()
            t.n.update(block=0, chunk=0)

            def claim():
                m = t.n["chunk"]
                t.up("chunk")
                b = m % RING
                if m >= RING:
                    pe.wait_ge(bank_taken[b], t.value(("round", b)))
                t.up(("round", b))
                return R[:, b, :]

            def weights():
                n = t.n["block"]
                pe.wait_ge(lo_done, t.up("block"))
                return n % SPLIT

            def three(o, w, hi, lo, start, stop, begins=False, end=None):
                i = pe.matmul(o, wh[w], hi, start=start, stop=False, skip_group_check=True)
                if begins:
                    i.then_inc(block_begun, 1)
                pe.matmul(o, wh[w], lo, start=False, stop=False, skip_group_check=True)
                i = pe.matmul(o, wl[w], hi, start=False, stop=stop, skip_group_check=True)
                if end is not None:
                    i.then_inc(end, 1)

            def dense(hi, lo, k_tiles=DC, ready=None):
                s = weights()
                for j in range(8 // k_tiles):
                    o = claim()
                    for k in range(k_tiles):
                        if ready is not None and j == 0:
                            ready(k)
                        a = (j * k_tiles + k) * P
                        three(o[:, 0:T], (slice(None), s, slice(a, a + P)), hi[:, k, :], lo[:, k, :], k == 0,
                              k == k_tiles - 1, begins=j == 0 and k == 0, end=chunk_ready if k == k_tiles - 1 else None)

            def tokens_major(hi, lo, per=2, tiles=DC):
                o = [claim(), claim()]
                for b in range(tiles // per):
                    s = weights()
                    for kk in range(per):
                        k = b * per + kk
                        for tt in range(TT):
                            last = k == tiles - 1
                            st, sl = k == 0, (slice(None), s, slice(kk * 512, kk * 512 + 512))
                            h, l = hi[:, k, tt * P:tt * P + P], lo[:, k, tt * P:tt * P + P]
                            i = pe.matmul(o[tt], h, wh[sl], start=st, stop=False, skip_group_check=True)
                            if kk == 0 and tt == 0:
                                i.then_inc(block_begun, 1)
                            pe.matmul(o[tt], l, wh[sl], start=False, stop=False, skip_group_check=True)
                            i = pe.matmul(o[tt], h, wl[sl], start=False, stop=last, skip_group_check=True)
                            if last:
                                i.then_inc(chunk_ready, 1)

            def from_dve(k=1):
                pe.wait_ge(dve_pe, t.up(dve_pe, k))

            def from_act(k=1):
                pe.wait_ge(act_pe, t.up(act_pe, k))

            def taken(m):
                pe.wait_ge(bank_taken[m % RING], m // RING + 1)

            def split_ready(k):
                from_dve()

            def ffn(ready):
                for b in range(4):
                    pe.matmul(Y[:, b, :], ZB[:, 0:P], ZB[:, :], start=True, stop=False, skip_group_check=True)

                def up_pair(ready=None):
                    dense(XH, XL, ready=ready)
                    dense(XH, XL)

                def down(f, end=None):
                    from_dve()
                    s = weights()
                    for c in range(DC):
                        three(Y[:, c // 2, (c % 2) * T:(c % 2) * T + T], (slice(None), s, slice(c * P, c * P + P)),
                              HH[:, f % 2, :], HL[:, f % 2, :], False, False, begins=c == 0,
                              end=end if c == DC - 1 else None)

                up_pair(ready)
                with pe.Fori(0, (FC - 2) // 4) as it:
                    t.enter(it, {"block": BODY, "chunk": 8, dve_pe: 4, **{("round", b): 2 for b in range(RING)}})
                    for j in range(4):
                        up_pair()
                        down(j)
                    t.leave((FC - 2) // 4)
                up_pair()
                down(FC - 2)
                down(FC - 1, end=y_ready)

            def stats(n, wait):
                o = claim()
                for c in range(n[0]):
                    wait(c)
                    i = pe.matmul(o[:, 0:T], ONES, n[1](c), start=c == 0, stop=c == n[0] - 1, skip_group_check=True)
                i.then_inc(chunk_ready, 1)

            def norm(n, src, mean, wait=None):
                if mean:
                    stats((n, src), wait)
                stats((n, lambda c: W8[:, c, :]), lambda c: from_act())

            def scores(u, a):
                S = Y[:, u % 2, :]
                if a["full"]:
                    for tt in range(TT):
                        i = pe.matmul(S[:, tt * T:tt * T + T], a["q"][:, tt * P:tt * P + P], a["k"], start=True, stop=True,
                                      skip_group_check=True)
                else:
                    pe.matmul(S[:, 0:3 * P], IDB[:, :], CAUS[:, :], start=True, stop=False, skip_group_check=True)
                    pe.matmul(S[:, 0:P], a["q"][:, 0:P], a["k"][:, 0:P], start=False, stop=True, skip_group_check=True)
                    i = pe.matmul(S[:, P:3 * P], a["q"][:, P:T], a["k"], start=False, stop=True, skip_group_check=True)
                i.then_inc(scores_ready, 1)

            def turn(u, a):
                from_dve()
                o, p = Y[:, 2, :], PR[:, u % 2, :]
                if a["full"]:
                    pairs = [(0, 0), (256, 128), (128, 256), (384, 384)]
                else:
                    pairs = [(0, 0), (128, 128), (256, 256)]
                for src, dst in pairs:
                    i = pe.transpose(o[:, dst:dst + P], p[:, src:src + P], IDF)
                i.then_inc(pt_ready, 1)

            def values(u, a):
                from_act()
                if a["opens"]:
                    if t.n.get("o", 0):
                        pe.wait_ge(o_taken, t.n["o"])
                    t.up("o")
                    if a.get("before"):
                        a["before"]()
                o = Y[a["row"]:a["row"] + a["width"], 3, :]
                pt = PTS[:, u % 2, :]
                pe.matmul(o[:, 0:T], a["v"](0), pt[:, 0:T], start=a["first"], stop=False, skip_group_check=True)
                lo = 0 if a["full"] else P
                i = pe.matmul(o[:, lo:T], a["v"](1), pt[:, T:T + T - lo], start=False, stop=True, skip_group_check=True)
                if a["last"]:
                    i.then_inc(o_ready, 1)

            def attention(units, filler):
                for u in range(len(units) + 2):
                    if u >= 2:
                        turn(u - 2, units[u - 2])
                    if u < len(units):
                        scores(u, units[u])
                        filler(u)
                    if u >= 2:
                        values(u - 2, units[u - 2])

            def mixer(l):
                dense(XH, XL, ready=split_ready)
                with pe.Fori(0, 2) as it:
                    t.enter(it, {"block": BODY, "chunk": BODY, **{("round", b): 3 for b in range(RING)}})
                    for _ in range(BODY):
                        dense(XH, XL)
                    t.leave(2)
                for _ in range(Z_N - 1 - 2 * BODY):
                    dense(XH, XL)
                last = t.n["chunk"] - 1
                taken(last)
                for c in (Z_KS, Z_KW, Z_Q, Z_Q + 1, Z_Q + 2, Z_Q + 3):
                    pe.matmul(claim()[:, 0:T], tab("perm64"), Z[:, c, :], start=True, stop=True).then_inc(chunk_ready, 1)
                o = claim()
                for tt in range(TT):
                    i = pe.transpose(o[:, tt * P:tt * P + P], Z[:, Z_MISC, tt * P:tt * P + P], IDF)
                i.then_inc(chunk_ready, 1)
                o = claim()
                for j, c in enumerate((Z_VS, Z_VW)):
                    for tt in range(TT):
                        a = (2 * j + tt) * P
                        i = pe.transpose(o[:, a:a + P], Z[:, c, tt * P:tt * P + P], IDF)
                i.then_inc(chunk_ready, 1)
                pe.wait_ge(wcmp_landed, 16 * (l + 1))
                from_dve()
                KX = W8[:, 0:2, :].rearrange("p a (l n) -> p (a l) n", n=CMP)
                VX = W8[:, 2:4, :].rearrange("p a (l n) -> p (a l) n", n=CMP)
                ks = [claim(), claim()]
                for g in range(2):
                    s = slice(64 * g, 64 * g + 64)
                    for j in range(32):
                        i = pe.matmul(ks[g][s, 0:CMP], WC[s, 0, j * 64:j * 64 + 64], KX[s, j, :], start=j == 0, stop=j == 31)
                    i.then_inc(chunk_ready, 1)
                vs = [claim(), claim()]
                for g in range(2):
                    s = slice(64 * g, 64 * g + 64)
                    for j in range(32):
                        i = pe.matmul(vs[g][0:CMP, s], VX[s, j, :], WC[s, 1, j * 64:j * 64 + 64], start=j == 0, stop=j == 31)
                    i.then_inc(chunk_ready, 1)
                from_dve()
                pe.matmul(claim()[:, 0:CMP], tab("perm64"), KC[:, 0, :], start=True, stop=True).then_inc(chunk_ready, 1)
                from_dve()
                pe.matmul(claim()[:, 0:P], tab("sel16", CMP), VCs[:, :], start=True, stop=True).then_inc(chunk_ready, 1)
                from_dve()
                for tt in range(TT):
                    for g in range(2):
                        s = slice(64 * g, 64 * g + 64)
                        o = claim()
                        pe.matmul(o[:, 0:4 * CMP], IDB[:, :], CMSK[:, tt, :], start=True, stop=False, skip_group_check=True)
                        for c in range(4):
                            i = pe.matmul(o[:, c * CMP:c * CMP + CMP], Z[s, Z_Q + c, tt * P:tt * P + P], KC[s, 1, :],
                                          start=False, stop=True, skip_group_check=True)
                        i.then_inc(chunk_ready, 1)
                o = claim()
                from_dve()
                for tt in range(TT):
                    i = pe.transpose(o[:, tt * P:tt * P + P], PR[:, 0, tt * P:tt * P + P], IDF)
                i.then_inc(chunk_ready, 1)
                norm(2, None, False)
                norm(1, None, False)
                from_dve(3)
                for _ in range(2):
                    dense(BH, BL, k_tiles=2)
                s = weights()
                for j in range(4):
                    three(claim()[:, 0:T], (slice(None), s, slice(j * P, j * P + P)), BH[:, 2, :], BL[:, 2, :], True, True,
                          begins=j == 0, end=chunk_ready)
                for tt in range(TT):
                    o, sl = claim(), (slice(None), s, slice(512, 1024))
                    h, lo = BH[:, 2, tt * P:tt * P + P], BL[:, 2, tt * P:tt * P + P]
                    pe.matmul(o, h, wh[sl], start=True, stop=False)
                    pe.matmul(o, lo, wh[sl], start=False, stop=False)
                    pe.matmul(o, h, wl[sl], start=False, stop=True).then_inc(chunk_ready, 1)
                from_dve()
                pe.matmul(claim()[:, 0:T], tab("place", 64), S1[0:64, :], start=True, stop=True).then_inc(chunk_ready, 1)
                norm(4, lambda c: Z[:, Z_V + c, :], True, lambda c: None)
                from_dve(4)
                for tt in range(TT):
                    o = claim()
                    for g in range(4):
                        i = pe.transpose(o[:, g * P:g * P + P], Z[:, Z_V + g, tt * P:tt * P + P], IDF)
                    i.then_inc(chunk_ready, 1)
                from_act(2)
                VT = W8[:, 4:8, :].rearrange("p (a b) t -> p a (b t)", a=2)
                for g in range(4):
                    o = claim()
                    a = g * P
                    for tt in range(TT):
                        c = slice(tt * P, tt * P + P)
                        pe.matmul(o[:, c], ONES[0:1, :], BSR[:, a:a + P], start=True, stop=False, skip_group_check=True)
                        i = pe.matmul(o[:, c], VT[:, tt, g * P:g * P + P], WS[:, g, :], start=False, stop=True,
                                      skip_group_check=True)
                    i.then_inc(chunk_ready, 1)
                from_dve()
                attention([mla_unit(h) for h in range(8)], lambda u: (dense(XH, XL), dense(XH, XL)))
                from_dve()
                for b in range(2):
                    for _ in range(4):
                        dense(BH[:, 4 * b:4 * b + 4, :], BL[:, 4 * b:4 * b + 4, :], k_tiles=4)
                units = [nsa_unit(u) for u in range(16)]
                for u in range(0, 16, 4):
                    units[u]["before"] = lambda c=u // 4: pe.matmul(
                        Y[:, 3, 0:T], VCB[:, c, :], S4[:, 0:T], start=True, stop=False, skip_group_check=True)
                attention(units, lambda u: dense(XH, XL))
                for b in range(2):
                    from_dve()
                    for _ in range(4):
                        dense(BH[:, 4 * b:4 * b + 4, :], BL[:, 4 * b:4 * b + 4, :], k_tiles=4)
                first = t.n["chunk"]
                for c in range(DC):
                    dense(XH, XL, ready=split_ready if c == 0 else None)
                return first

            def cross():
                from_dve(DC + 1)
                for _ in range(4):
                    dense(BH, BL)
                tokens_major(BH, BL)
                for c in range(4):
                    dense(XH, XL)
                from_act()
                attention([cross_unit(h) for h in range(4)], lambda u: None)
                from_dve()
                first = t.n["chunk"]
                for _ in range(4):
                    dense(BH, BL, k_tiles=4)
                return first

            def gla():
                c = mixer0_chunks()
                for j in range(c["n"]):
                    dense(XH, XL, ready=split_ready if j == 0 else None)
                taken(t.n["chunk"] - 1)
                gu = cols["gate_up"][0]
                for j in range(2):
                    pe.matmul(claim()[:, 0:T], SM[0:16, gu + j * P:gu + j * P + P], Z[0:16, c["lr"], :], start=True,
                              stop=True).then_inc(chunk_ready, 1)
                tokens_major(XH, XL)
                o = claim()
                from_dve()
                for j in range(2):
                    for tt in range(TT):
                        i = pe.transpose(o[:, (tt * 2 + j) * P:(tt * 2 + j) * P + P], Z[:, c["k"] + j, tt * P:tt * P + P], IDF)
                i.then_inc(chunk_ready, 1)
                from_act()
                KT = PR[:, 0, :].rearrange("p (t c) -> p t c", t=2)
                V = Z[:, 26:30, :].rearrange("p (a b) t -> p a (b t)", a=2)
                for n in range(4):
                    o, s = claim(), slice(64 * (n % 2), 64 * (n % 2) + 64)
                    for h in range(4):
                        d = slice(64 * (h % 2), 64 * (h % 2) + 64)
                        i = pe.matmul(o[d, (h // 2) * P:(h // 2) * P + P], KT[s, n // 2, h * 64:h * 64 + 64],
                                      V[s, n // 2, h * P:h * P + P], start=True, stop=True, skip_group_check=True)
                    i.then_inc(chunk_ready, 1)
                from_dve()
                ST = Z[:, 30:34, :].rearrange("p n (c v) -> p n c v", c=2)
                for h in range(4):
                    o, d = claim(), slice(64 * (h % 2), 64 * (h % 2) + 64)
                    for n in range(4):
                        i = pe.matmul(o[:, n * 64:n * 64 + 64], ST[d, n, h // 2, :], Z[d, c["q"] + h // 2, n * 64:n * 64 + 64],
                                      start=True, stop=True, skip_group_check=True)
                    i.then_inc(chunk_ready, 1)
                for j in range(2):
                    o = claim()
                    from_act()
                    pe.matmul(o, ONES, W8[:, 2 * j:2 * j + 2, :].rearrange("p a t -> p (a t)"), start=True,
                              stop=True).then_inc(chunk_ready, 1)
                from_dve()
                s = weights()
                for j in range(8):
                    three(claim()[:, 0:T], (slice(None), s, slice(j * P, j * P + P)), BH[:, j % 4, :], BL[:, j % 4, :], True, True,
                          begins=j == 0, end=chunk_ready)
                from_dve()
                first = t.n["chunk"]
                for _ in range(DC):
                    dense(BH, BL)
                return first

            def hgrn():
                for j in range(24):
                    dense(XH, XL, ready=split_ready if j == 0 else None)
                for _ in range(2):
                    tokens_major(XH, XL)
                KT = G[:, 0, :, :].rearrange("p (t c) k -> p t (c k)", t=2)
                V = G[:, 1, :, :].rearrange("p (t c) k -> p t (c k)", t=2)
                for tt in range(TT):
                    for b in range(2):
                        o = claim()
                        if tt == 0 and b == 0:
                            from_dve()
                        for h in range(4):
                            i = pe.transpose(o[:, h * P:h * P + P], Z[:, 8 + 4 * b + h, tt * P:tt * P + P], IDF)
                        i.then_inc(chunk_ready, 1)
                from_act()
                for n in range(4):
                    s = slice(64 * (n % 2), 64 * (n % 2) + 64)
                    for b in range(2):
                        o = claim()
                        for h in range(4):
                            k = slice((4 * b + h) * P, (4 * b + h) * P + P)
                            i = pe.matmul(o[:, h * P:h * P + P], KT[s, n // 2, k], V[s, n // 2, k], start=True, stop=True,
                                          skip_group_check=True)
                        i.then_inc(chunk_ready, 1)
                    from_dve()
                    for h in range(8):
                        i = pe.matmul(Y[:, h // 2, (h % 2) * T + n * 64:(h % 2) * T + n * 64 + 64],
                                      M[:, 4 * (n % 2):4 * (n % 2) + 4, :].rearrange("p a t -> p (a t)")[:, h * P:h * P + P],
                                      Z[:, h, n * 64:n * 64 + 64], start=True, stop=True, skip_group_check=True)
                    i.then_inc(y_ready, 1)
                for j in range(4):
                    o = claim()
                    from_act()
                    pe.matmul(o, ONES, W8[:, 2 * j:2 * j + 2, :].rearrange("p a t -> p (a t)"), start=True,
                              stop=True).then_inc(chunk_ready, 1)
                from_dve()
                first = t.n["chunk"]
                for _ in range(DC):
                    dense(BH, BL)
                return first

            pe.wait_ge(small_landed, 48)
            pe.wait_ge(pool_const, 4)
            from_act()
            xs = lambda c: X[:, c, :]
            first_split = lambda k: from_dve() if k == 0 else None
            ffn(first_split)
            for l in range(DEPTH):
                norm(DC, xs, True, lambda c: from_dve())
                first = mixer(l)
                norm(DC, xs, True, lambda c, f=first: taken(f + c))
                first = cross()
                norm(DC, xs, True, lambda c, f=first: taken(f + c))
                ffn(split_ready)
                norm(DC, xs, True, lambda c: from_dve())
                if l + 1 < DEPTH:
                    ffn(split_ready)
            from_dve(DC)
            for l in range(DEPTH):
                norm(DC, None, False)
                ffn(split_ready)
                norm(DC, None, False)
                gla() if l == 0 else hgrn()
                norm(DC, None, False)
                ffn(split_ready)
                norm(DC, None, False)
                from_dve(DC + 1)
                for _ in range(2):
                    dense(BH, BL, k_tiles=2)
                for c in range(DC):
                    dense(XH, XL)
            norm(DC, None, False)
            assert t.n["block"] == NB, (t.n["block"], NB)

        @block.scalar
        def _(act):
            t = Tally()
            t.n.update(hi=0, chunk=0, begun=1)

            def split_next():
                n = t.n["hi"]
                if t.it is None and n >= NB:
                    return
                act.wait_ge(raw_landed[n % RAW], t.up(("raw", n % RAW), 16))
                if n >= SPLIT:
                    act.wait_ge(block_begun, t.up("begun"))
                t.up("hi")
                act.activation(wh[:, n % SPLIT, :], raw[:, n % RAW, :], ACT.Copy).then_inc(hi_done, 1)

            def step(i):
                i.then_inc(act_step, 1)
                act.wait_ge(act_step, t.up(act_step))

            def give_dve(i):
                i.then_inc(act_dve, 1)
                act.wait_ge(act_dve, t.up(act_dve))

            def give_pe(i):
                i.then_inc(act_pe, 1)
                act.wait_ge(act_pe, t.up(act_pe))

            def from_dve(k=1):
                act.wait_ge(dve_act, t.up(dve_act, k))

            def chunk():
                m = t.n["chunk"]
                act.wait_ge(chunk_ready, t.up("chunk"))
                t.up(("round", m % RING))
                return m, R[:, m % RING, :]

            def skip(k):
                for _ in range(k):
                    m = t.n["chunk"]
                    t.up("chunk")
                    t.up(("round", m % RING))

            def take(i, m, wait=True):
                i.then_inc(bank_taken[m % RING], 1)
                if wait:
                    act.wait_ge(bank_taken[m % RING], t.value(("round", m % RING)))

            def ffn():
                def hidden(j):
                    m, o = chunk()
                    give_dve(act.activation(EB[:, j % 2, :], o[:, 0:T], ACT.Tanh, scale=0.5))
                    skip(1)

                def pair(j):
                    split_next()
                    hidden(j)
                    split_next()

                pair(0)
                per = {"hi": BODY, "chunk": 8, "begun": BODY, act_dve: 4, **{("round", b): 2 for b in range(RING)},
                       **{("raw", r): 32 for r in range(RAW)}}
                with act.Fori(0, (FC - 2) // 4) as it:
                    t.enter(it, per)
                    for j in range(4):
                        pair(j + 1)
                        split_next()
                    t.leave((FC - 2) // 4)
                pair(FC - 1)
                split_next()
                split_next()

            def rstd(n, scale, eps, width=T):
                m, o = chunk()
                step(act.activation(S2[:, 0:width], o[:, 0:width], ACT.Ln, scale=scale, bias=EPS[:, eps:eps + 1]))
                give_dve(act.activation(S3[:, 0:width], S2[:, 0:width], ACT.Exp, scale=-0.5))

            def norm(n, src, mean, scale, eps, bias, hi):
                if mean:
                    skip(1)
                for c in range(n):
                    from_dve()
                    give_pe(act.activation(W8[:, c, :], src(c), ACT.Square))
                rstd(n, scale, eps)
                if hi is not None:
                    for c in range(n):
                        from_dve()
                        b = 0.0 if bias is None else bias(c)
                        give_dve(act.activation(hi[:, c, :], W8[:, c, :], ACT.Identity, bias=b))

            def softmax(u, a):
                from_dve()
                S, b = Y[:, u % 2, :], u % 2
                cuts = (0, 256, 512) if a["full"] else (0, 128, 384)
                for tt in range(TT):
                    i = act.activation(PR[:, b, cuts[tt]:cuts[tt + 1]], S[:, cuts[tt]:cuts[tt + 1]], ACT.Exp, scale=a["scale"],
                                       bias=nm[:, b, tt:tt + 1], accum_out=ls[:, b, tt:tt + 1])
                    step(i) if tt == 0 else give_dve(i)

            def turned(u, a):
                act.wait_ge(pt_ready, t.up(pt_ready))
                w = 512 if a["full"] else 384
                give_pe(act.activation(PTS[:, u % 2, 0:w], Y[:, 2, 0:w], ACT.Copy))

            def attention(units, filler):
                for u in range(len(units) + 2):
                    if u >= 2:
                        turned(u - 2, units[u - 2])
                    if u < len(units):
                        softmax(u, units[u])
                        filler(u)

            def plain(dst, scale=1.0, wait=False):
                m, o = chunk()
                take(act.activation(dst, o[:, 0:T], ACT.Copy, scale=scale), m, wait)

            def mixer(l):
                def z(c):
                    split_next()
                    m, o = chunk()
                    take(act.activation(Z[:, c, :], o[:, 0:T], ACT.Identity, bias=col(f"b_in{l}", c)), m, wait=False)

                for c in range(Z_N):
                    z(c)
                skip(6)
                m, o = chunk()
                take(act.activation(GT[:, :, :], o[:, 0:T].rearrange("p (a b) -> p a b", a=2)[:, :, 64:88], ACT.Exp, scale=-1.0), m)
                m, o = chunk()
                take(act.activation(VSW[:, :, :].rearrange("p a b -> p (a b)"), o[:, :], ACT.Copy), m)
                skip(6)
                skip(4)
                for tt in range(TT):
                    from_dve()
                    v = PR[:, 0, tt * P:tt * P + P]
                    give_dve(act.activation(v, v, ACT.Exp, scale=0.125))
                m, o = chunk()
                take(act.activation(S4[:, 0:T], o[:, 0:T], ACT.Copy), m)
                norm(2, lambda c: Z[:, Z_QL + c, :], False, 1.0 / 256, 1, None, BH)
                norm(1, lambda c: Z[:, Z_KVL, :], False, 1.0 / 128, 1, None, BH[:, 2:3, :])
                split_next()
                split_next()
                split_next()
                skip(8)
                for j in range(4):
                    m, o = chunk()
                    step(act.activation(KM[0:64, 2 * j, :], o[0:64, 0:T], ACT.Copy))
                    take(act.activation(KM[64:128, 2 * j + 1, :], o[64:128, 0:T], ACT.Copy), m)
                for tt in range(TT):
                    m, o = chunk()
                    take(act.activation(VM[:, tt, :], o, ACT.Copy), m)
                m, o = chunk()
                step(act.activation(KM[64:128, 0:8:2, :], o[64:128, 0:T].unsqueeze(1).to_broadcast([64, 4, T]), ACT.Copy))
                take(act.activation(KM[0:64, 1:8:2, :], o[0:64, 0:T].unsqueeze(1).to_broadcast([64, 4, T]), ACT.Copy), m)
                norm(4, lambda c: Z[:, Z_V + c, :], True, 1.0 / 512, 0, None, None)
                VT = W8[:, 4:8, :].rearrange("p (a b) t -> p a (b t)", a=2)
                for tt in range(TT):
                    m, o = chunk()
                    take(act.activation(VT[:, tt, :], o, ACT.Copy), m)
                    act.sem_inc(act_pe, 1)
                    t.up(act_pe)
                skip(4)

                def gate(b, c):
                    split_next()
                    m, o = chunk()
                    j = b * DC + c
                    take(act.activation(G[:, b % 2, c, :], o[:, 0:T], ACT.Tanh, scale=0.5, bias=NB_IN[:, j:j + 1]), m, wait=False)

                attention([mla_unit(h) for h in range(8)], lambda u: (gate(u // 4, 2 * u % 8), gate(u // 4, (2 * u + 1) % 8)))
                for _ in range(8):
                    split_next()
                skip(16)
                from_dve()
                attention([nsa_unit(u) for u in range(16)], lambda u: gate(2 + u // 8, u % 8))
                for _ in range(8):
                    split_next()
                skip(16)
                for c in range(DC):
                    from_dve()
                    give_dve(act.activation(XH[:, c, :], M[:, c, :], ACT.Copy, scale=0.5))
                act.dma_start(G[:, 0, :, :], mem_in).then_inc(in_landed, 16)
                for _ in range(DC):
                    split_next()
                skip(DC)

            def cross():
                from_dve()
                give_dve(act.activation(BH[:, :, :], G[:, 0, :, :], ACT.Copy))
                for c in range(4):
                    split_next()
                    plain(Z[:, c, :])
                for _ in range(4):
                    split_next()
                for tt in range(TT):
                    m, o = chunk()
                    take(act.activation(Z[:, 8 + 2 * tt:10 + 2 * tt, :].rearrange("p a t -> p (a t)"), o, ACT.Copy), m, wait=False)
                for c in range(4):
                    split_next()
                    m, o = chunk()
                    i = act.activation(Z[:, 4 + c, :], o[:, 0:T], ACT.Copy)
                    take(i, m)
                act.sem_inc(act_pe, 1)
                t.up(act_pe)
                attention([cross_unit(h) for h in range(4)], lambda u: None)
                for _ in range(4):
                    split_next()
                skip(DC)

            def logsig_parts(e, n):
                step(act.activation(e, e, ACT.Exp, scale=-1.0))
                give_dve(act.activation(e, e, ACT.Ln, bias=EPS[:, 2:3]))

            def gla():
                c = mixer0_chunks()
                for j in range(c["n"]):
                    split_next()
                    plain(Z[:, j, :], 0.125 if c["q"] <= j < c["k"] else 0.5 if c["g"] <= j < c["lr"] else 1.0)
                skip(2)
                for _ in range(4):
                    split_next()
                from_dve()
                logsig_parts(Z[:, 20:22, :], 2)
                from_dve()
                step(act.activation(Z[:, 20:22, :], Z[:, 20:22, :], ACT.Exp))
                give_dve(act.activation(c8[:, 0, :], c8[:, 0, :], ACT.Exp))
                for tt in range(TT):
                    m, o = chunk()
                    take(act.activation(Z[:, 26 + 2 * tt:28 + 2 * tt, :].rearrange("p a t -> p (a t)"), o, ACT.Copy), m)
                m, o = chunk()
                take(act.activation(PR[:, 0, :], o, ACT.Copy), m)
                act.sem_inc(act_pe, 1)
                t.up(act_pe)
                skip(4)
                for h in range(4):
                    m, o = chunk()
                    take(act.activation(O[:, h, :], o[:, 0:T], ACT.Copy), m)
                for j in range(2):
                    give_pe(act.activation(W8[:, 2 * j:2 * j + 2, :], O[:, 2 * j:2 * j + 2, :], ACT.Square))
                for j in range(2):
                    rstd(1, 1.0 / 128, 1, 512)
                    from_dve()
                give_dve(act.activation(W8[:, 4:8, :], Z[:, c["g"]:c["g"] + 4, :], ACT.Tanh))
                from_dve()
                logsig_parts(c8[:, 1, 0:4], 4)
                from_dve()
                give_dve(act.activation(BH[:, 0:4, :], Z[:, 22:26, :], ACT.Copy))
                split_next()
                for j in range(8):
                    m, o = chunk()
                    take(act.activation(W8[:, j, :], o[:, 0:T], ACT.Tanh, scale=0.5, bias=c8[:, 2 + j // 4, j % 4:j % 4 + 1]), m)
                act.sem_inc(act_dve, 1)
                t.up(act_dve)
                from_dve()
                step(act.activation(Z[:, 18:22, :], W8[:, 0:4, :], ACT.Exp))
                give_dve(act.activation(W8[:, 0:4, :], W8[:, 0:4, :], ACT.Tanh))
                from_dve()
                step(act.activation(W8[:, 0:4, :], W8[:, 0:4, :], ACT.Ln))
                give_dve(act.activation(W8[:, 0:4, :], W8[:, 0:4, :], ACT.Exp, scale=0.5))
                from_dve()
                give_dve(act.activation(W8[:, 0:4, :], W8[:, 0:4, :], ACT.Tanh, scale=0.7978845608028654))
                from_dve()
                step(act.activation(BH[:, 0:4, :], O[:, :, :], ACT.Copy))
                give_dve(act.activation(BH[:, 4:8, :], Z[:, 18:22, :], ACT.Copy))
                for _ in range(DC):
                    split_next()
                skip(DC)

            def hgrn():
                for j in range(24):
                    split_next()
                    plain(Z[:, j, :], 1.0 if 8 <= j < 16 else 0.5, wait=j == 23)
                act.sem_inc(act_dve, 1)
                t.up(act_dve)
                for _ in range(8):
                    split_next()
                for b in range(2):
                    for tt in range(TT):
                        m, o = chunk()
                        take(act.activation(G[:, 1, :, :].rearrange("p (t b c) k -> p t b (c k)", t=2, b=2)[:, tt, b, :],
                                            o, ACT.Copy), m)
                q, f = Z[:, 0:8, :], Z[:, 8:16, :]
                step(act.activation(M[:, :, :], f, ACT.Tanh, scale=0.5))
                give_dve(act.activation(W8[:, :, :], q, ACT.Tanh))
                from_dve()
                give_dve(act.activation(W8[:, :, :], W8[:, :, :], ACT.Ln))
                from_dve()
                step(act.activation(M[:, :, :], M[:, :, :], ACT.Exp))
                give_dve(act.activation(c8[:, 0:4, :], c8[:, 0:4, :], ACT.Exp))
                for j in range(4):
                    m, o = chunk()
                    take(act.activation(G[:, 0, 2 * j:2 * j + 2, :].rearrange("p a t -> p (a t)"), o, ACT.Copy), m)
                act.sem_inc(act_pe, 1)
                t.up(act_pe)
                skip(8)
                act.wait_ge(y_ready, t.up(y_ready, 0) + 4)
                t.up(y_ready, 4)
                for b in range(4):
                    step(act.activation(Z[:, 24 + 2 * b:26 + 2 * b, :].rearrange("p a t -> p (a t)"), Y[:, b, :], ACT.Copy))
                    give_pe(act.activation(W8[:, 2 * b:2 * b + 2, :].rearrange("p a t -> p (a t)"), Y[:, b, :], ACT.Square))
                for j in range(4):
                    rstd(1, 1.0 / 128, 1, 512)
                    from_dve()
                give_dve(act.activation(W8[:, :, :], Z[:, 16:24, :], ACT.Tanh))
                from_dve()
                give_dve(act.activation(BH[:, :, :], Z[:, 24:32, :], ACT.Copy))
                for _ in range(DC):
                    split_next()
                skip(DC)

            act.wait_ge(small_landed, 48)
            step(act.activation(CAUS[:, :], Z[:, 0:2, :].rearrange("p a t -> p (a t)")[:, 0:3 * P], ACT.Copy))
            step(act.activation(IDB[:, :], IDF, ACT.Copy))
            give_pe(act.activation(CMSK[:, :, :].rearrange("p a b -> p (a b)"), Z[:, 1, P:T], ACT.Copy))
            act.wait_ge(pool_const, 4)
            for _ in range(SPLIT - 1):
                split_next()
            from_dve()
            give_dve(act.activation(LB[:, 0:2, :], LB[:, 0:2, :], ACT.Exp))
            act.wait_ge(x_landed, 16)
            give_dve(act.activation(XH[:, :, :], X[:, :, :], ACT.Copy))
            xs = lambda c: X[:, c, :]
            ffn()
            t.up(y_ready)
            for l in range(DEPTH):
                ln = lambda i: norm(DC, xs, True, 1.0 / D, 0, lambda c: col(f"ln{i}_b{l}", c), XH)
                ln(1)
                act.dma_start(WC[:, :, :], wcmp[l]).then_inc(wcmp_landed, 16)
                act.dma_start(WS[:, :, :], mix_w[l]).then_inc(mix_landed, 16)
                act.dma_start(BSR, mix_b[l]).then_inc(mix_landed, 16)
                mixer(l)
                ln(2)
                cross()
                ln(3)
                ffn()
                t.up(y_ready)
                if l + 1 < DEPTH:
                    ln(4)
                else:
                    norm(DC, xs, True, 1.0 / D, 0, None, None)
                if l + 1 < DEPTH:
                    ffn()
                    t.up(y_ready)
            for l in range(DEPTH):
                rms = lambda: norm(DC, xs, False, 1.0 / D, 1, None, XH)
                rms()
                ffn()
                t.up(y_ready)
                rms()
                gla() if l == 0 else hgrn()
                rms()
                act.dma_start(G[:, 0, 0:2, :], p_in[l]).then_inc(in_landed, 16)
                ffn()
                t.up(y_ready)
                rms()
                from_dve()
                give_dve(act.activation(BH[:, 0:2, :], G[:, 0, 0:2, :], ACT.Copy))
                for j in range(2):
                    split_next()
                    for i in range(4):
                        plain(M[:, 4 * j + i, :], wait=True)
                for c in range(DC):
                    split_next()
                    m, o = chunk()
                    take(act.activation(W8[:, c, :], o[:, 0:T], ACT.Tanh, scale=0.5), m)
                    act.sem_inc(act_dve, 1)
                    t.up(act_dve)
            norm(DC, xs, False, 1.0 / D, 1, None, None)
            from_dve()
            act.dma_start(out, X[:, :, :]).then_inc(out_stored, 16)
            act.wait_ge(out_stored, 16)

        @block.vector
        def _(dve):
            t = Tally()
            t.n.update(chunk=0)

            def step(i):
                i.then_inc(dve_step, 1)
                dve.wait_ge(dve_step, t.up(dve_step))

            def give_act(i):
                i.then_inc(dve_act, 1)
                dve.wait_ge(dve_act, t.up(dve_act))

            def give_pe(i):
                i.then_inc(dve_pe, 1)
                dve.wait_ge(dve_pe, t.up(dve_pe))

            def from_act(k=1):
                dve.wait_ge(act_dve, t.up(act_dve, k))

            def chunk():
                m = t.n["chunk"]
                dve.wait_ge(chunk_ready, t.up("chunk"))
                t.up(("round", m % RING))
                return m, R[:, m % RING, :]

            def skip(k):
                for _ in range(k):
                    m = t.n["chunk"]
                    t.up("chunk")
                    t.up(("round", m % RING))

            def take(i, m):
                i.then_inc(bank_taken[m % RING], 1)
                dve.wait_ge(bank_taken[m % RING], t.value(("round", m % RING)))

            def taken():
                m = t.n["chunk"] - 1
                dve.wait_ge(bank_taken[m % RING], t.value(("round", m % RING)))

            tt_, ts_, stt = dve.tensor_tensor, dve.tensor_scalar, dve.scalar_tensor_tensor

            def ffn(scale):
                def hidden(j):
                    b = j % 2
                    e, h = EB[:, b, :], HID[:, b, :]
                    from_act()
                    m, o = chunk()
                    take(stt(e, e, 1.0, o[:, 0:T], ALU.add, ALU.mult), m)
                    m, o = chunk()
                    take(stt(h, e, 0.5 * scale, o[:, 0:T], ALU.mult, ALU.mult), m)
                    step(dve.tensor_copy(HH[:, b, :], h))
                    give_pe(tt_(HL[:, b, :], h, HH[:, b, :].bitcast(F32), ALU.subtract))

                hidden(0)
                with dve.Fori(0, (FC - 2) // 4) as it:
                    t.enter(it, {"chunk": 8, dve_step: 4, dve_pe: 4, act_dve: 4, **{("round", b): 2 for b in range(RING)}})
                    for j in range(4):
                        hidden(j + 1)
                    t.leave((FC - 2) // 4)
                hidden(FC - 1)

            def ybank(c):
                return Y[:, c // 2, (c % 2) * T:(c % 2) * T + T]

            def add_y(alpha, give):
                dve.wait_ge(y_ready, t.up(y_ready))
                for c in range(DC):
                    give(stt(X[:, c, :], X[:, c, :], alpha, ybank(c), ALU.mult, ALU.add))

            def add_chunks(alpha, signal_act=False):
                for c in range(DC):
                    m, o = chunk()
                    take(stt(X[:, c, :], X[:, c, :], alpha, o[:, 0:T], ALU.mult, ALU.add), m)
                    if signal_act:
                        dve.sem_inc(dve_act, 1)
                        t.up(dve_act)

            def sharpen(scale, eps, width=T):
                from_act()
                m, o = chunk()
                y, v, w = S3[:, 0:width], S2[:, 0:width], S4[:, 0:width] if width > T else S4[:, T:T + width]
                take(ts_(v, o[:, 0:width], scale, eps, ALU.mult, ALU.add), m)
                step(tt_(w, y, y, ALU.mult))
                step(tt_(w, w, v, ALU.mult))
                step(ts_(w, w, -0.5, 1.5, ALU.mult, ALU.add))
                step(tt_(y, y, w, ALU.mult))

            def norm(n, src, mean, scale, eps, gain, bias, hi, lo, squares=False, dst=None):
                if mean:
                    m, o = chunk()
                    take(ts_(S1[:, :], o[:, 0:T], scale, None, ALU.mult), m)
                    for c in range(n):
                        give_act(tt_(src(c), src(c), S1[:, :], ALU.subtract))
                elif squares:
                    for c in range(n):
                        dve.sem_inc(dve_act, 1)
                        t.up(dve_act)
                sharpen(scale, eps)
                for c in range(n):
                    i = stt(W8[:, c, :], src(c), gain(c), S3[:, 0:T], ALU.mult, ALU.mult)
                    give_act(i) if hi is not None else step(i)
                    if hi is None:
                        d = src(c) if dst is None else dst(c)
                        b = 0.0 if bias is None else bias(c)
                        give_pe(ts_(d, W8[:, c, :], b, None, ALU.add))
                        continue
                    if bias is not None:
                        step(ts_(src(c), W8[:, c, :], bias(c), None, ALU.add))
                    from_act()
                    s = W8[:, c, :] if bias is None else src(c)
                    give_pe(tt_(lo[:, c, :], s, hi[:, c, :].bitcast(F32), ALU.subtract))

            def softmax(u, a):
                dve.wait_ge(scores_ready, t.up(scores_ready))
                S, b = Y[:, u % 2, :], u % 2
                cuts = (0, 256, 512) if a["full"] else (0, 128, 384)
                for tt in range(TT):
                    step(dve.tensor_reduce(mx[:, b, tt:tt + 1], S[:, cuts[tt]:cuts[tt + 1]], AX.X, ALU.max))
                give_act(ts_(nm[:, b, :], mx[:, b, :], -a["scale"], None, ALU.mult))

            def normalise(u, a):
                b = u % 2
                cuts = (0, 256, 512) if a["full"] else (0, 128, 384)
                from_act()
                step(dve.reciprocal(rl[:, b, :], ls[:, b, :]))
                if a["gate"] is not None:
                    step(tt_(rl[:, b, :], rl[:, b, :], GT[:, :, a["gate"]], ALU.mult))
                for tt in range(TT):
                    v = PR[:, b, cuts[tt]:cuts[tt + 1]]
                    i = ts_(v, v, rl[:, b, tt:tt + 1], None, ALU.mult)
                    step(i) if tt == 0 else give_pe(i)

            def attention(units, filler):
                for u in range(len(units) + 2):
                    if u < len(units):
                        softmax(u, units[u])
                        filler(u)
                    if 1 <= u <= len(units):
                        normalise(u - 1, units[u - 1])
                    if u >= 2 and units[u - 2]["last"]:
                        dve.wait_ge(o_ready, t.up(o_ready))
                        dve.tensor_copy(O[:, units[u - 2]["c"], :], Y[:, 3, 0:T]).then_inc(o_taken, 1)
                        dve.wait_ge(o_taken, t.up(o_taken))

            def split(hi, lo, src):
                step(dve.tensor_copy(hi, src))
                give_pe(tt_(lo, src, hi.bitcast(F32), ALU.subtract))

            def one_over_one_plus(a):
                step(ts_(a, a, 1.0, None, ALU.add))
                step(dve.reciprocal(a, a))

            def mixer(l):
                skip(Z_N)
                step(ts_(NB_IN[:, :], col(f"b_in{l}", Z_N, Z_GATES), 0.5, None, ALU.mult))
                dve.wait_ge(mix_landed, 32 * (l + 1))
                step(tt_(WS[:, :, :], WS[:, :, :], tab("tri").unsqueeze(1).to_broadcast([P, 4, P]), ALU.mult))
                taken()
                for c in (Z_KS, Z_KW, Z_Q, Z_Q + 1, Z_Q + 2, Z_Q + 3):
                    m, o = chunk()
                    take(tt_(S1[:, :], o[:, 0:T], tab("sin64"), ALU.mult), m)
                    step(tt_(Z[:, c, :], Z[:, c, :], tab("cos64"), ALU.mult))
                    step(tt_(Z[:, c, :], Z[:, c, :], S1[:, :], ALU.add))
                skip(2)
                taken()
                one_over_one_plus(GT[:, :, :])
                for i, (zc, pe_) in enumerate(((Z_KC, "pe_k"), (Z_VC, "pe_v"))):
                    w = W8[:, 2 * i:2 * i + 2, :].rearrange("p a (l n) -> p (a l) n", n=CMP)
                    v = Z[:, zc, :].rearrange("p (n s) -> p s n", s=16)
                    step(dve.memset(w[:, :, N_CMP:CMP], 0.0))
                    for half in range(2):
                        term = col(f"{pe_}{l}", 16 * half, 16).unsqueeze(2).to_broadcast([P, 16, N_CMP])
                        step(tt_(w[:, 16 * half:16 * half + 16, 0:N_CMP], v[:, :, half:half + N_CMP], term, ALU.add))
                dve.sem_inc(dve_pe, 1)
                t.up(dve_pe)
                for g in range(2):
                    s = slice(64 * g, 64 * g + 64)
                    m, o = chunk()
                    take(dve.tensor_copy(KC[s, 0, :], o[s, 0:CMP]), m)
                dve.sem_inc(dve_pe, 1)
                t.up(dve_pe)
                for g in range(2):
                    s = slice(64 * g, 64 * g + 64)
                    m, o = chunk()
                    take(dve.tensor_copy(VCs[:, s], o[0:CMP, s]), m)
                dve.sem_inc(dve_pe, 1)
                t.up(dve_pe)
                m, o = chunk()
                take(tt_(S1[:, 0:CMP], o[:, 0:CMP], tab("csin"), ALU.mult), m)
                step(tt_(KC[:, 1, :], KC[:, 0, :], tab("ccos"), ALU.mult))
                give_pe(tt_(KC[:, 1, :], KC[:, 1, :], S1[:, 0:CMP], ALU.add))
                m, o = chunk()
                take(tt_(VCB[:, :, :], o[:, 0:P].unsqueeze(1).to_broadcast([P, 4, P]),
                         tab("vmask").rearrange("p (a b) -> p a b", a=4), ALU.mult), m)
                for tt in range(TT):
                    v = PR[:, 0, tt * P:tt * P + P].rearrange("p (h n) -> p h n", n=CMP)
                    for g in range(2):
                        m, o = chunk()
                        sc = o[:, 0:4 * CMP].rearrange("p (h n) -> p h n", n=CMP)
                        step(dve.tensor_reduce(c8[:, 0, 4 * g:4 * g + 4], sc, AX.X, ALU.max))
                        take(tt_(v[:, 4 * g:4 * g + 4, :], sc, c8[:, 0, 4 * g:4 * g + 4].unsqueeze(2).to_broadcast([P, 4, CMP]),
                                 ALU.subtract), m)
                    dve.sem_inc(dve_act, 1)
                    t.up(dve_act)
                    from_act()
                    step(dve.tensor_reduce(c8[:, 1, :], v, AX.X, ALU.add))
                    step(dve.reciprocal(c8[:, 1, :], c8[:, 1, :]))
                    step(tt_(c8[:, 1, :], c8[:, 1, :], GT[:, tt, 0:24:3], ALU.mult))
                    ok = tab("valid")[:, tt * CMP:tt * CMP + CMP].unsqueeze(1).to_broadcast([P, 8, CMP])
                    step(tt_(v, v, ok, ALU.mult))
                    step(tt_(v, v, c8[:, 1, :].unsqueeze(2).to_broadcast([P, 8, CMP]), ALU.mult))
                dve.sem_inc(dve_pe, 1)
                t.up(dve_pe)
                skip(1)
                cv = lambda k, c: col(f"conv{l}", 4 * k + c)
                step(tt_(Z[:, Z_CC:Z_CC + 4, :], Z[:, Z_CC:Z_CC + 4, :], Z[:, Z_CH:Z_CH + 4, :], ALU.mult))
                for c in range(4):
                    p, y = Z[:, Z_CC + c, :], Z[:, Z_CH + c, :]
                    step(ts_(y, p, cv(2, c), None, ALU.mult))
                    step(stt(y[:, 1:T], p[:, 0:T - 1], cv(1, c), y[:, 1:T], ALU.mult, ALU.add))
                    step(stt(y[:, 2:T], p[:, 0:T - 2], cv(0, c), y[:, 2:T], ALU.mult, ALU.add))
                y = Z[:, Z_CH:Z_CH + 4, :]
                step(tt_(y, y, Z[:, Z_CB:Z_CB + 4, :], ALU.mult))
                step(dve.tensor_copy(BH[:, 4:8, :], y))
                step(tt_(BL[:, 4:8, :], y, BH[:, 4:8, :].bitcast(F32), ALU.subtract))
                norm(2, lambda c: Z[:, Z_QL + c, :], False, 1.0 / 256, RMS_EPS, lambda c: col(f"qn{l}", c), None, BH, BL, squares=True)
                norm(1, lambda c: Z[:, Z_KVL, :], False, 1.0 / 128, RMS_EPS, lambda c: col(f"kvn{l}"), None, BH[:, 2:3, :],
                     BL[:, 2:3, :], squares=True)
                for h in range(8):
                    m, o = chunk()
                    take(tt_(QM[:, h, :], o[:, 0:T], tab("tqe" if h % 2 == 0 else "tqo"), ALU.mult), m)
                give_pe(tt_(S1[0:64, :], Z[0:64, Z_MISC, :], tab("tqo")[0:64, :], ALU.mult))
                skip(7)
                taken()
                norm(4, lambda c: Z[:, Z_V + c, :], True, 1.0 / 512, LN_EPS, lambda c: col(f"gln_g{l}", c),
                     lambda c: col(f"gln_b{l}", c), None, None)
                skip(2)
                for g in range(4):
                    m, o = chunk()
                    u = Z[:, Z_U + g, :]
                    take(tt_(u, u, o[:, 0:T], ALU.mult), m)
                u = Z[:, Z_U:Z_U + 4, :]
                step(dve.tensor_copy(BH[:, 0:4, :], u))
                step(tt_(BL[:, 0:4, :], u, BH[:, 0:4, :].bitcast(F32), ALU.subtract))
                dve.sem_inc(dve_pe, 1)
                t.up(dve_pe)
                attention([mla_unit(h) for h in range(8)], lambda u: skip(2))
                dve.sem_inc(dve_pe, 1)
                t.up(dve_pe)
                taken()

                def merge(b):
                    for c in range(DC):
                        m, o = chunk()
                        g = G[:, b % 2, c, :]
                        if b == 0:
                            take(stt(M[:, c, :], g, 1.0, o[:, 0:T], ALU.add, ALU.mult), m)
                        else:
                            take(stt(g, g, 1.0, o[:, 0:T], ALU.add, ALU.mult), m)
                            i = tt_(M[:, c, :], M[:, c, :], g, ALU.add)
                            give_act(i) if b == 3 else step(i)

                merge(0)
                merge(1)
                dve.sem_inc(dve_act, 1)
                t.up(dve_act)
                step(dve.tensor_copy(BH[:, 0:4, :], O[:, :, :]))
                step(tt_(BL[:, 0:4, :], O[:, :, :], BH[:, 0:4, :].bitcast(F32), ALU.subtract))
                attention([nsa_unit(u) for u in range(16)], lambda u: skip(1))
                dve.sem_inc(dve_pe, 1)
                t.up(dve_pe)
                split(BH[:, 4:8, :], BL[:, 4:8, :], O[:, :, :])
                taken()
                merge(2)
                merge(3)
                for c in range(DC):
                    from_act()
                    give_pe(stt(XL[:, c, :], M[:, c, :], 0.5, XH[:, c, :].bitcast(F32), ALU.mult, ALU.subtract))

            def cross():
                dve.wait_ge(in_landed, t.up(in_landed, 16))
                dve.sem_inc(dve_act, 1)
                t.up(dve_act)
                from_act()
                give_pe(tt_(BL[:, :, :], G[:, 0, :, :], BH[:, :, :].bitcast(F32), ALU.subtract))
                skip(10)
                attention([cross_unit(h) for h in range(4)], lambda u: None)
                split(BH[:, 0:4, :], BL[:, 0:4, :], O[:, :, :])

            def logsig(x, e, big):
                give_act(stt(e, x, -1.0, x, ALU.mult, ALU.max))
                step(ts_(x, x, 0.0, None, ALU.min))
                from_act()
                step(tt_(x, x, e, ALU.subtract))

            def gla():
                c = mixer0_chunks()
                skip(c["n"])
                for j in range(2):
                    m, o = chunk()
                    take(ts_(Z[:, 18 + j, :], o[:, 0:T], col("gate_b", j), None, ALU.add), m)
                logsig(Z[:, 18:20, :], Z[:, 20:22, :], None)
                step(ts_(Z[:, 18:20, :], Z[:, 18:20, :], 1.0 / 16.0, None, ALU.mult))
                for j in range(2):
                    step(dve.tensor_tensor_scan(Z[:, 20 + j, :], tab("reset"), Z[:, 18 + j, :], 0.0, ALU.mult, ALU.add))
                cum = Z[:, 20:22, :].rearrange("p c (n s) -> p (c n) s", s=64)
                step(dve.tensor_copy(c8[:, 0, :], cum[:, :, 63]))
                give_act(tt_(cum, c8[:, 0, :].unsqueeze(2).to_broadcast([P, 8, 64]), cum, ALU.subtract))
                from_act()
                give_pe(tt_(Z[:, c["k"]:c["k"] + 2, :], Z[:, c["k"]:c["k"] + 2, :], Z[:, 20:22, :], ALU.mult))
                skip(3)
                ST = Z[:, 30:34, :].rearrange("p n (c v) -> p n c v", c=2)
                for n in range(4):
                    m, o = chunk()
                    v = o[:, 0:T].rearrange("p (c v) -> p c v", c=2)
                    if n == 0:
                        take(dve.tensor_copy(ST[:, 0, :, :], v), m)
                        continue
                    for j in range(2):
                        i = stt(ST[:, n, j, :], ST[:, n - 1, j, :], c8[:, 0, 4 * j + n:4 * j + n + 1], v[:, j, :], ALU.mult, ALU.add)
                        step(i) if j == 0 else take(i, m)
                dve.sem_inc(dve_pe, 1)
                t.up(dve_pe)
                for j in range(4):
                    x, y = Z[:, c["xr"] + j, :], Z[:, 22 + j, :]
                    step(ts_(y, x, col("lconv", 12 + j), col("lconv_b", j), ALU.mult, ALU.add))
                    for d in range(1, 4):
                        step(stt(y[:, d:T], x[:, 0:T - d], col("lconv", 4 * (3 - d) + j), y[:, d:T], ALU.mult, ALU.add))
                skip(4)
                for j in range(2):
                    sharpen(1.0 / 128, RMS_EPS, 512)
                    o2 = O[:, 2 * j:2 * j + 2, :].rearrange("p a t -> p (a t)")
                    give_act(stt(o2, o2, col("gla_hn"), S3[:, :], ALU.mult, ALU.mult))
                from_act()
                g = Z[:, c["g"]:c["g"] + 4, :]
                step(stt(g, W8[:, 4:8, :], 1.0, g, ALU.add, ALU.mult))
                step(tt_(O[:, :, :], O[:, :, :], g, ALU.mult))
                step(dve.tensor_copy(c8[:, 4, 0:4], col("lam", 0, 4)))
                step(ts_(c8[:, 2, 0:4], col("lru_ba", 0, 4), 0.5, None, ALU.mult))
                step(ts_(c8[:, 3, 0:4], col("lru_bx", 0, 4), 0.5, None, ALU.mult))
                logsig(c8[:, 4, 0:4], c8[:, 1, 0:4], None)
                step(ts_(c8[:, 4, 0:4], c8[:, 4, 0:4], 4.0, None, ALU.mult))
                dve.sem_inc(dve_act, 1)
                t.up(dve_act)
                from_act()
                give_pe(tt_(BL[:, 0:4, :], Z[:, 22:26, :], BH[:, 0:4, :].bitcast(F32), ALU.subtract))
                skip(8)
                from_act()
                xr = Z[:, 22:26, :]
                for j in range(4):
                    i = ts_(W8[:, j, :], W8[:, j, :], 1.0, c8[:, 4, j:j + 1], ALU.add, ALU.mult)
                    step(i) if j < 3 else give_act(i)
                from_act()
                w = W8[:, 0:4, :]
                v = W8[:, 4:8, :]
                step(stt(xr, v, 1.0, xr, ALU.add, ALU.mult))
                a = Z[:, 18:22, :]
                step(tt_(v, a, a, ALU.mult))
                step(stt(w, v, 1.0, w, ALU.add, ALU.mult))
                give_act(ts_(w, w, -1.0, 1e-19, ALU.mult, ALU.max))
                from_act()
                step(stt(xr, xr, 0.5, w, ALU.mult, ALU.mult))
                for j in range(4):
                    step(dve.tensor_tensor_scan(Z[:, 26 + j, :], Z[:, 18 + j, :], Z[:, 22 + j, :], 0.0, ALU.mult, ALU.add))
                xg = Z[:, c["xg"]:c["xg"] + 4, :]
                step(tt_(w, xg, xg, ALU.mult))
                step(ts_(w, w, 0.044715, 1.0, ALU.mult, ALU.add))
                give_act(tt_(w, w, xg, ALU.mult))
                from_act()
                step(stt(w, w, 1.0, xg, ALU.add, ALU.mult))
                give_act(stt(Z[:, 18:22, :], Z[:, 26:30, :], 0.5, w, ALU.mult, ALU.mult))
                from_act()
                step(tt_(BL[:, 0:4, :], O[:, :, :], BH[:, 0:4, :].bitcast(F32), ALU.subtract))
                give_pe(tt_(BL[:, 4:8, :], Z[:, 18:22, :], BH[:, 4:8, :].bitcast(F32), ALU.subtract))
                add_chunks(1.0, signal_act=True)

            def hgrn():
                skip(24)
                from_act()
                skip(4)
                from_act()
                q, f = Z[:, 0:8, :], Z[:, 8:16, :]
                step(stt(q, W8[:, :, :], 1.0, q, ALU.add, ALU.mult))
                for c in range(DC):
                    th = M[:, c, :]
                    step(ts_(W8[:, c, :], th, LB[:, 1, c:c + 1], LB[:, 0, c:c + 1], ALU.mult, ALU.add))
                    step(ts_(f[:, c, :], th, LB[:, 2, c:c + 1], LB[:, 1, c:c + 1], ALU.mult, ALU.add))
                give_act(ts_(W8[:, :, :], W8[:, :, :], 2.0 ** -64, None, ALU.max))
                from_act()
                for c in range(DC):
                    step(dve.tensor_tensor_scan(M[:, c, :], tab("reset"), W8[:, c, :], 0.0, ALU.mult, ALU.add))
                cum = M[:, :, :].rearrange("p c (n s) -> p (c n) s", s=64)
                tot = c8[:, 0:4, :].rearrange("p a b -> p (a b)")
                step(dve.tensor_copy(tot, cum[:, :, 63]))
                give_act(tt_(cum, tot.unsqueeze(2).to_broadcast([P, 32, 64]), cum, ALU.subtract))
                from_act()
                give_pe(tt_(f, f, M[:, :, :], ALU.mult))
                skip(4)
                for n in range(4):
                    S = M[:, 4 * (n % 2):4 * (n % 2) + 4, :].rearrange("p a t -> p (a t)")
                    Sp = M[:, 4 * ((n + 1) % 2):4 * ((n + 1) % 2) + 4, :].rearrange("p a t -> p (a t)")
                    for b in range(2):
                        m, o = chunk()
                        if n == 0:
                            take(dve.tensor_copy(S[:, b * 512:b * 512 + 512], o), m)
                            continue
                        for h in range(4):
                            k = slice((4 * b + h) * P, (4 * b + h) * P + P)
                            hh = 4 * b + h
                            i = stt(S[:, k], Sp[:, k], tot[:, 4 * hh + n:4 * hh + n + 1], o[:, h * P:h * P + P], ALU.mult, ALU.add)
                            step(i) if h < 3 else take(i, m)
                    dve.sem_inc(dve_pe, 1)
                    t.up(dve_pe)
                t.up(y_ready, 4)
                for j in range(4):
                    sharpen(1.0 / 128, RMS_EPS, 512)
                    o2 = Z[:, 24 + 2 * j:26 + 2 * j, :].rearrange("p a t -> p (a t)")
                    give_act(stt(o2, o2, col("hg_hn"), S3[:, :], ALU.mult, ALU.mult))
                from_act()
                g, o8 = Z[:, 16:24, :], Z[:, 24:32, :]
                step(stt(g, W8[:, :, :], 1.0, g, ALU.add, ALU.mult))
                give_act(tt_(o8, o8, g, ALU.mult))
                from_act()
                give_pe(tt_(BL[:, :, :], o8, BH[:, :, :].bitcast(F32), ALU.subtract))
                add_chunks(1.0, signal_act=True)

            dve.wait_ge(x_landed, 16)
            dve.wait_ge(small_landed, 48)
            l0, l1 = col("lb0", 0, DC), col("lb1", 0, DC)
            step(tt_(LB[:, 2, :], l0, l1, ALU.max))
            step(tt_(LB[:, 0, :], l1, LB[:, 2, :], ALU.subtract))
            give_act(tt_(LB[:, 1, :], l0, LB[:, 2, :], ALU.subtract))
            from_act()
            step(tt_(LB[:, 2, :], LB[:, 0, :], LB[:, 1, :], ALU.add))
            step(dve.reciprocal(LB[:, 2, :], LB[:, 2, :]))
            step(tt_(LB[:, 0, :], LB[:, 0, :], LB[:, 2, :], ALU.mult))
            step(stt(LB[:, 1, :], LB[:, 1, :], 0.5, LB[:, 2, :], ALU.mult, ALU.mult))
            step(tt_(LB[:, 0, :], LB[:, 0, :], LB[:, 1, :], ALU.add))
            step(ts_(LB[:, 2, :], LB[:, 1, :], -1.0, None, ALU.mult))
            from_act()
            give_pe(tt_(XL[:, :, :], X[:, :, :], XH[:, :, :].bitcast(F32), ALU.subtract))
            xs = lambda c: X[:, c, :]
            ffn(0.5)
            for l in range(DEPTH):
                ln = lambda i: norm(DC, xs, True, 1.0 / D, LN_EPS, lambda c: col(f"ln{i}_g{l}", c),
                                    lambda c: col(f"ln{i}_b{l}", c), XH, XL)
                add_y(ALPHA, give_pe)
                ln(1)
                mixer(l)
                add_chunks(ALPHA)
                ln(2)
                cross()
                add_chunks(ALPHA)
                ln(3)
                ffn(0.5)
                add_y(ALPHA, give_pe)
                if l + 1 < DEPTH:
                    ln(4)
                else:
                    norm(DC, xs, True, 1.0 / D, LN_EPS, lambda c: col(f"ln4_g{l}", c), lambda c: col(f"ln4_b{l}", c), None, None)
                if l + 1 < DEPTH:
                    ffn(0.5)
            for l in range(DEPTH):
                def rms(gain, squares=False):
                    norm(DC, xs, False, 1.0 / D, RMS_EPS, lambda c: col(gain, c), None, XH, XL, squares=squares)
                rms(f"ffn_g{l}_0", squares=l == 0)
                ffn(0.5)
                add_y(1.0, give_act)
                rms(f"mix_g{l}")
                gla() if l == 0 else hgrn()
                rms(f"ffn_g{l}_1")
                ffn(0.5)
                add_y(1.0, give_act)
                rms(f"ple_g{l}")
                dve.wait_ge(in_landed, t.up(in_landed, 16))
                dve.sem_inc(dve_act, 1)
                t.up(dve_act)
                from_act()
                give_pe(tt_(BL[:, 0:2, :], G[:, 0, 0:2, :], BH[:, 0:2, :].bitcast(F32), ALU.subtract))
                skip(8)
                for c in range(DC):
                    skip(1)
                    from_act()
                    step(stt(M[:, c, :], W8[:, c, :], 1.0, M[:, c, :], ALU.add, ALU.mult))
                    give_act(stt(X[:, c, :], M[:, c, :], 0.5, X[:, c, :], ALU.mult, ALU.add))
            norm(DC, xs, False, 1.0 / D, RMS_EPS, lambda c: col("final_g", c), None, None, None)
            dve.sem_inc(dve_act, 1)


def in_columns():
    at = np.cumsum([0, 512, 512, 512, 512, 512, 256, 128, 32, 512] + [128] * 6 + [24] + [D] * 4)
    u, v, cb, cc, ch, ql, kvl, kr, q, kc, vc, ks, vs, kw, vw, gt, ga = at[:17]
    run = lambda a, n: list(range(a, a + n))
    idx = []
    for a in (kc, vc, ks, vs, kw, vw):
        idx += run(a, P)
    for c in range(4):
        idx += run(q + 64 * c, 64) + run(q + 64 * (4 + c), 64)
    idx += run(kr, 32) + run(kr + 16, 16) + run(kr, 16) + run(gt, 24) + [-1] * 40
    idx += run(ql, 256) + run(kvl, P)
    for a in (u, v, cb, cc, ch):
        idx += run(a, 512)
    idx += run(ga, Z_GATES * P)
    return np.array(idx)


def columns_of(w, idx):
    w = np.concatenate([w, np.zeros(w.shape[:-1] + (1,), w.dtype)], -1)
    return w[..., idx]


def chunk_blocks(w):
    k, n = w.shape
    t = w.reshape(k // P, P, n // P, P).transpose(2, 0, 1, 3).reshape(-1, 8, P, P)
    return t.transpose(0, 2, 1, 3).reshape(-1, P, 1024)


def token_blocks(w):
    return w.reshape(4, 2, P, 512).transpose(0, 2, 1, 3).reshape(4, P, 1024)


def ffn_blocks(w1, w3, w2):
    a, b, c = chunk_blocks(w1), chunk_blocks(w3), w2.reshape(FC, P, 1024)
    out = np.empty((3 * FC, P, 1024), w1.dtype)
    out[0], out[1] = a[0], b[0]
    body = out[2:2 + 3 * (FC - 1)].reshape(FC - 1, 3, P, 1024)
    body[:, 0], body[:, 1], body[:, 2] = a[1:], b[1:], c[:-1]
    out[-1] = c[-1]
    return out


def pack_stream(a):
    parts = []
    for l in range(DEPTH):
        parts.append(ffn_blocks(a["ffn1_w1"][l], a["ffn1_w3"][l], a["ffn1_w2"][l]))
        w = columns_of(a["w_in"][l], in_columns())
        parts.append(chunk_blocks(w[:, :Z_N * P]))
        idx, run = [], lambda s, n: list(range(s, s + n))
        for h in range(8):
            nope, r = run(96 * h, 64), 96 * h + 64
            rope = run(r, 32) + run(r + 16, 16) + run(r, 16)
            idx += nope + rope if h % 2 == 0 else rope + nope
        parts.append(chunk_blocks(a["mla_wuq"][l][:, idx]))
        kv = a["mla_wukv"][l].reshape(P, 8, 2, 64).transpose(0, 2, 1, 3).reshape(1, P, 1024)
        parts.append(kv)
        gates = w[:, Z_N * P:]
        half = 2 * D
        parts += [chunk_blocks(gates[:, :half]), chunk_blocks(a["gmlp_wout"][l]), chunk_blocks(a["conv_wout"][l]),
                  chunk_blocks(gates[:, half:]), chunk_blocks(a["mla_wout"][l])]
        rows = np.concatenate([np.r_[64 * c:64 * c + 64, 64 * (4 + c):64 * (4 + c) + 64] for c in range(4)])
        parts += [chunk_blocks(a["nsa_wout"][l][rows]), chunk_blocks(a["w_o"][l])]
        parts += [chunk_blocks(a["xattn_wk"][l]), token_blocks(a["xattn_wv"][l]), chunk_blocks(a["xattn_wq"][l]),
                  chunk_blocks(a["xattn_wo"][l])]
        parts.append(ffn_blocks(a["ffn2_w1"][l], a["ffn2_w3"][l], a["ffn2_w2"][l]))
    for l in range(DEPTH):
        for i in range(2):
            parts.append(ffn_blocks(a["ffn_w1_2"][l, i], a["ffn_w3_2"][l, i], a["ffn_w2_2"][l, i]))
            if i:
                parts += [chunk_blocks(a["ple_proj_2"][l]), chunk_blocks(a["ple_gate_2"][l])]
            elif l == 0:
                w = a["m0_w_in_2"][0]
                part = lambda s, n, w=w: w[:, s:s + n]
                lr = columns_of(w, np.r_[1536:1552, [-1] * 112])
                fm = np.concatenate([part(1552, 512), part(2064, 512), part(0, 256), part(256, 256), part(1024, 512), lr], 1)
                parts += [chunk_blocks(fm), token_blocks(part(512, 512))]
                tiles = np.zeros((8, P, P), w.dtype)
                for n, name in enumerate(("lru_wa_2", "lru_wx_2")):
                    g = a[name][0]
                    tiles[4 * n:4 * n + 4, :64, :64] = g[0::2]
                    tiles[4 * n:4 * n + 4, 64:, 64:] = g[1::2]
                parts += [tiles.transpose(1, 0, 2).reshape(1, P, 1024), chunk_blocks(a["m0_w_out_2"][0])]
            else:
                w = a["m1_w_in_2"][0]
                parts += [chunk_blocks(np.concatenate([w[:, :2 * D], w[:, 3 * D:]], 1)), token_blocks(w[:, 2 * D:2 * D + 512]),
                          token_blocks(w[:, 2 * D + 512:3 * D]), chunk_blocks(a["m1_w_out_2"][0])]
    return np.concatenate(parts)


def pack_small(a):
    plan, n = column_plan()
    out = np.zeros((P, n), np.float32)

    def put(name, v):
        v = v.reshape(-1, P).T if v.ndim == 1 else v
        out[:v.shape[0], plan[name][0]:plan[name][0] + plan[name][1]] = v

    dup = lambda v: np.concatenate([v, v])
    for l in range(DEPTH):
        for i in range(1, 5):
            for k in "gb":
                put(f"ln{i}_{k}{l}", a[f"ln{i}_{k}"][l])
        put(f"b_in{l}", columns_of(a["b_in"][l], in_columns()))
        put(f"gln_g{l}", a["gmlp_ln_g"][l])
        put(f"gln_b{l}", a["gmlp_ln_b"][l])
        put(f"conv{l}", a["conv_w"][l].reshape(-1))
        put(f"qn{l}", a["mla_qnorm_g"][l])
        put(f"kvn{l}", a["mla_kvnorm_g"][l])
        put(f"pe_k{l}", dup(a["nsa_pe_k"][l].T))
        put(f"pe_v{l}", dup(a["nsa_pe_v"][l].T))
        for i in range(2):
            put(f"ffn_g{l}_{i}", a["ffn_norm_2"][l, i])
        put(f"mix_g{l}", a["mix_norm_2"][l])
        put(f"ple_g{l}", a["ple_norm_2"][l])
        put(f"lb{l}", a["hgrn_lb_logits_2"][l])
    put("final_g", a["final_norm_2"])
    put("gate_up", a["gla_gate_up_2"][0])
    for name, key in (("gate_b", "gla_gate_bias_2"), ("gla_hn", "gla_head_norm_2"), ("lconv_b", "lru_conv_b_2"),
                      ("lru_ba", "lru_ba_2"), ("lru_bx", "lru_bx_2"), ("lam", "lru_lambda_2"), ("hg_hn", "hgrn_head_norm_2")):
        put(name, a[key][0])
    put("lconv", a["lru_conv_w_2"][0].reshape(-1))
    return out


def feature_major(v):
    return np.ascontiguousarray(v.T.reshape(-1, P, T).transpose(1, 0, 2))


def layout(a):
    table, masks = tables()
    d = {
        "stream": pack_stream(a), "small": pack_small(a), "table": table, "masks": masks,
        "mix_w": a["gmlp_ws"].transpose(0, 3, 1, 2).reshape(DEPTH, P, 4 * P),
        "mix_b": a["gmlp_bs"].reshape(DEPTH, 1, 4 * P),
        "wcmp": np.stack([np.stack([np.concatenate([w[l].transpose(1, 0, 2).reshape(64, 2048)] * 2)
                                    for w in (a["nsa_wcmp_k"], a["nsa_wcmp_v"])], 1) for l in range(DEPTH)]),
        "x": feature_major(a["x"][0]), "mem": feature_major(a["mem"][0]),
        "p": np.stack([feature_major(a["p_2"][l, 0]) for l in range(DEPTH)]),
    }
    return {k: np.ascontiguousarray(v) for k, v in d.items()}


def kernel(**inputs):
    import concourse.bacc as bacc
    from concourse.bass_utils import run_bass_kernel_spmd

    arrays = layout({k: np.asarray(v) for k, v in inputs.items()})
    nc = bacc.Bacc("TRN2", target_bir_lowering=False, num_devices=1)
    args = [nc.dram_tensor(f"in_{k}", v.shape, F32, kind="ExternalInput").ap() for k, v in arrays.items()]
    out = nc.dram_tensor("out_dram", (P, DC, T), F32, kind="ExternalOutput").ap()
    build_program(nc, *args, out)
    r = run_bass_kernel_spmd(nc, [{f"in_{k}": v for k, v in arrays.items()}], core_ids=[0])
    got = r.results[0]["out_dram"]
    return np.ascontiguousarray(got.transpose(1, 0, 2).reshape(D, T).T).reshape(1, T, D)
```
